# Optimizing a Trainium2 kernel written in Bass

```python
import math
import jax
import jax.numpy as jnp
from jax import lax
import numpy as np

D_MODEL = 2048
BATCH = 1
SEQ = 256
DEPTH = 2

FFN_HIDDEN = ((8 * D_MODEL + 3 * 256 - 1) // (3 * 256)) * 256

SC_WIDTH = D_MODEL // 2
SC_KERNEL = 3
DN_HEADS = 8
DN_HEAD_DIM = 128
DN_WIDTH = DN_HEADS * DN_HEAD_DIM
DN_CONV = 4
DN_CHUNK = 64
HY_WIDTHS = [SC_WIDTH, SC_WIDTH, SC_WIDTH, 3 * DN_WIDTH, DN_WIDTH, DN_HEADS, DN_HEADS]
HY_COLS = sum(HY_WIDTHS)

NSA_HEADS = 16
NSA_KV_HEADS = 4
NSA_HEAD_DIM = 128
NSA_KV_WIDTH = NSA_KV_HEADS * NSA_HEAD_DIM
CMP_BLOCK = 32
CMP_STRIDE = 16
CMP_HIDDEN = 2 * NSA_HEAD_DIM
SEL_BLOCK = 64
N_SELECT = 16
WINDOW = 512
SEL_Q_BLOCK = 16
WIN_Q_BLOCK = 128
NSA_WIDTHS = [NSA_HEADS * NSA_HEAD_DIM] + [NSA_KV_WIDTH] * 6 + [3 * NSA_HEADS]
NSA_COLS = sum(NSA_WIDTHS)
ATTN_SCALE = NSA_HEAD_DIM ** -0.5

ROPE_THETA = 10000.0
LN_EPS = 1e-5
NORM_EPS = 1e-6
NEG_INF = -1e30
DEEPNORM_ALPHA = (2 * DEPTH) ** 0.25
DEEPNORM_BETA = (8 * DEPTH) ** -0.25
N_EVEN = (DEPTH + 1) // 2
N_ODD = DEPTH // 2

kernel_name = 'hybrid_shortconv_deltanet_nsa_deepnorm'

def _split_cols(t, widths):
    cuts = [int(c) for c in np.cumsum(widths)[:-1]]
    return jnp.split(t, cuts, axis=-1)

def layer_norm(x, g, b):
    xf = x.astype(jnp.float32)
    mu = jnp.mean(xf, axis=-1, keepdims=True)
    var = jnp.mean(jnp.square(xf - mu), axis=-1, keepdims=True)
    return ((xf - mu) * lax.rsqrt(var + LN_EPS) * g + b).astype(x.dtype)

def causal_depthwise_conv(x, w):
    k, s = w.shape[0], x.shape[1]
    xp = jnp.pad(x, ((0, 0), (k - 1, 0), (0, 0)))
    out = xp[:, 0:s] * w[0]
    for j in range(1, k):
        out = out + xp[:, j:j + s] * w[j]
    return out

def l2norm(t):
    return t * lax.rsqrt(jnp.sum(jnp.square(t), axis=-1, keepdims=True) + NORM_EPS)

def rope_angles(pos):
    half = NSA_HEAD_DIM // 2
    inv = jnp.power(ROPE_THETA, -jnp.arange(half, dtype=jnp.float32) / half)
    ang = pos.astype(jnp.float32)[..., None] * inv
    return jnp.cos(ang), jnp.sin(ang)

def apply_rope(x, cos, sin):
    x1, x2 = jnp.split(x.astype(jnp.float32), 2, axis=-1)
    return jnp.concatenate([x1 * cos - x2 * sin, x2 * cos + x1 * sin], axis=-1).astype(x.dtype)

def gated_delta_rule(q, k, v, g, beta):
    b, h, s, dk = q.shape
    dv = v.shape[-1]
    c = DN_CHUNK
    n = s // c
    q = q * dk ** -0.5
    qc = q.reshape(b, h, n, c, dk)
    kc = k.reshape(b, h, n, c, dk)
    vc = v.reshape(b, h, n, c, dv)
    bc = beta.reshape(b, h, n, c, 1)
    gc = jnp.cumsum(g.reshape(b, h, n, c), axis=-1)
    incl = jnp.tril(jnp.ones((c, c), dtype=bool))
    strict = jnp.tril(jnp.ones((c, c), dtype=bool), -1)
    decay = jnp.where(incl, jnp.exp(jnp.where(incl, gc[..., :, None] - gc[..., None, :], 0.0)), 0.0)
    kbeta = kc * bc
    a_mat = jnp.where(strict, jnp.einsum('bhnid,bhnjd->bhnij', kbeta, kc) * decay, 0.0)
    rhs = jnp.concatenate([vc * bc, kbeta * jnp.exp(gc)[..., None]], axis=-1)
    sol = lax.linalg.triangular_solve(jnp.eye(c, dtype=a_mat.dtype) + a_mat, rhs,
                                      left_side=True, lower=True, unit_diagonal=True)
    u, w = sol[..., :dv], sol[..., dv:]
    intra = jnp.einsum('bhnid,bhnjd->bhnij', qc, kc) * decay
    q_dec = qc * jnp.exp(gc)[..., None]
    k_dec = kc * jnp.exp(gc[..., -1:] - gc)[..., None]
    g_last = jnp.exp(gc[..., -1])

    def step(state, inp):
        q_i, k_i, u_i, w_i, a_i, gl = inp
        v_new = u_i - jnp.einsum('bhcd,bhde->bhce', w_i, state)
        o = jnp.einsum('bhcd,bhde->bhce', q_i, state) + jnp.einsum('bhij,bhje->bhie', a_i, v_new)
        state = state * gl[..., None, None] + jnp.einsum('bhcd,bhce->bhde', k_i, v_new)
        return state, o

    xs = (jnp.moveaxis(q_dec, 2, 0), jnp.moveaxis(k_dec, 2, 0), jnp.moveaxis(u, 2, 0),
          jnp.moveaxis(w, 2, 0), jnp.moveaxis(intra, 2, 0), jnp.moveaxis(g_last, 2, 0))
    _, o = lax.scan(step, jnp.zeros((b, h, dk, dv), q.dtype), xs)
    return jnp.moveaxis(o, 0, 2).reshape(b, h, s, dv)

def conv_deltanet_mixer(x, w_in, sc_conv_w, dn_conv_w, a_log, dt_bias, norm_w, w_out):
    b, s, _ = x.shape
    f32 = jnp.float32
    sc_b, sc_c, sc_h, dn_qkv, dn_z, dn_b, dn_a = _split_cols(x @ w_in, HY_WIDTHS)
    y_sc = sc_b * causal_depthwise_conv(sc_c * sc_h, sc_conv_w)
    qkv = jax.nn.silu(causal_depthwise_conv(dn_qkv, dn_conv_w))
    q, k, v = jnp.split(qkv, 3, axis=-1)

    def heads(t):
        return t.reshape(b, s, DN_HEADS, DN_HEAD_DIM).transpose(0, 2, 1, 3).astype(f32)

    q, k, v, z = l2norm(heads(q)), l2norm(heads(k)), heads(v), heads(dn_z)
    beta = jax.nn.sigmoid(dn_b.astype(f32)).transpose(0, 2, 1)
    g = (-jnp.exp(a_log.astype(f32)) * jax.nn.softplus(dn_a.astype(f32) + dt_bias.astype(f32))).transpose(0, 2, 1)
    o = gated_delta_rule(q, k, v, g, beta)
    o = o * lax.rsqrt(jnp.mean(jnp.square(o), axis=-1, keepdims=True) + NORM_EPS) * norm_w * jax.nn.silu(z)
    y_dn = o.transpose(0, 2, 1, 3).reshape(b, s, DN_WIDTH).astype(x.dtype)
    return jnp.concatenate([y_sc, y_dn], axis=-1) @ w_out

def compress_blocks(kt, pos_emb, w1, w2):
    b, s, g_, dh = kt.shape
    r = CMP_BLOCK // CMP_STRIDE
    n_sub = s // CMP_STRIDE
    n_cmp = n_sub - r + 1
    sub = kt.reshape(b, n_sub, CMP_STRIDE, g_, dh)
    blocks = jnp.concatenate([sub[:, i:i + n_cmp] for i in range(r)], axis=2)
    blocks = blocks + pos_emb[:, None, :]
    blocks = blocks.transpose(0, 3, 1, 2, 4).reshape(b, g_, n_cmp, CMP_BLOCK * dh)
    return jax.nn.gelu(blocks @ w1) @ w2

def select_blocks(p_grp, s):
    rs = SEL_BLOCK // CMP_STRIDE
    rc = CMP_BLOCK // CMP_STRIDE
    n_sel = s // SEL_BLOCK
    n_cmp = p_grp.shape[-1]
    length = rs * n_sel + rc - 1
    pp = jnp.pad(p_grp, ((0, 0), (0, 0), (0, 0), (rc - 1, length - (rc - 1) - n_cmp)))
    score = None
    for m in range(rs):
        for n in range(rc):
            term = pp[..., m + n:m + n + rs * n_sel:rs]
            score = term if score is None else score + term
    t = jnp.arange(s)[:, None]
    j = jnp.arange(n_sel)[None, :]
    cur = t // SEL_BLOCK
    forced = (j == 0) | (j == cur) | (j == cur - 1)
    future = j * SEL_BLOCK > t
    score = jnp.where(forced, jnp.inf, jnp.where(future, -jnp.inf, score))
    _, idx = lax.top_k(score, min(N_SELECT, n_sel))
    return idx

def selected_attention(q, k, v, idx):
    b, g_, hpg, s, dh = q.shape
    ksel = idx.shape[-1]
    n_sel = s // SEL_BLOCK
    nq = s // SEL_Q_BLOCK
    k_blk = k.reshape(b, g_, n_sel, SEL_BLOCK, dh)
    v_blk = v.reshape(b, g_, n_sel, SEL_BLOCK, dh)
    bi = jnp.arange(b)[:, None, None, None]
    gi = jnp.arange(g_)[None, :, None, None]
    offs = jnp.arange(SEL_BLOCK)
    q_chunks = jnp.moveaxis(q.reshape(b, g_, hpg, nq, SEL_Q_BLOCK, dh), 3, 0)
    i_chunks = jnp.moveaxis(idx.reshape(b, g_, nq, SEL_Q_BLOCK, ksel), 2, 0)

    def one_chunk(args):
        qb, ib, c = args
        kg = k_blk[bi, gi, ib]
        vg = v_blk[bi, gi, ib]
        kpos = ib[..., None] * SEL_BLOCK + offs
        tq = c * SEL_Q_BLOCK + jnp.arange(SEL_Q_BLOCK)
        valid = (kpos <= tq[:, None, None])[:, :, None]
        sc = jnp.einsum('bghqd,bgqkld->bghqkl', qb, kg).astype(jnp.float32) * ATTN_SCALE
        p = jax.nn.softmax(jnp.where(valid, sc, NEG_INF), axis=(-2, -1))
        return jnp.einsum('bghqkl,bgqkld->bghqd', p.astype(vg.dtype), vg)

    o = lax.map(one_chunk, (q_chunks, i_chunks, jnp.arange(nq)))
    return jnp.moveaxis(o, 0, 3).reshape(b, g_, hpg, s, dh)

def window_attention(q, k, v):
    b, g_, hpg, s, dh = q.shape
    nq = s // WIN_Q_BLOCK
    span = WIN_Q_BLOCK + WINDOW
    kp = jnp.pad(k, ((0, 0), (0, 0), (WINDOW, 0), (0, 0)))
    vp = jnp.pad(v, ((0, 0), (0, 0), (WINDOW, 0), (0, 0)))
    q_chunks = jnp.moveaxis(q.reshape(b, g_, hpg, nq, WIN_Q_BLOCK, dh), 3, 0)

    def one_chunk(args):
        qb, c = args
        start = c * WIN_Q_BLOCK
        kb = lax.dynamic_slice_in_dim(kp, start, span, axis=2)
        vb = lax.dynamic_slice_in_dim(vp, start, span, axis=2)
        kpos = start - WINDOW + jnp.arange(span)
        tq = start + jnp.arange(WIN_Q_BLOCK)
        valid = (kpos[None, :] <= tq[:, None]) & (kpos[None, :] > tq[:, None] - WINDOW) & (kpos[None, :] >= 0)
        sc = jnp.einsum('bghqd,bgkd->bghqk', qb, kb).astype(jnp.float32) * ATTN_SCALE
        p = jax.nn.softmax(jnp.where(valid, sc, NEG_INF), axis=-1)
        return jnp.einsum('bghqk,bgkd->bghqd', p.astype(vb.dtype), vb)

    o = lax.map(one_chunk, (q_chunks, jnp.arange(nq)))
    return jnp.moveaxis(o, 0, 3).reshape(b, g_, hpg, s, dh)

def nsa_mixer(x, positions, w_in, cmp_pos_k, cmp_w1_k, cmp_w2_k, cmp_pos_v, cmp_w1_v, cmp_w2_v, w_out):
    b, s, _ = x.shape
    hq, g_, dh = NSA_HEADS, NSA_KV_HEADS, NSA_HEAD_DIM
    hpg = hq // g_
    q, k_c, v_c, k_s, v_s, k_w, v_w, gates = _split_cols(x @ w_in, NSA_WIDTHS)
    cos, sin = rope_angles(positions)
    cos, sin = cos[:, :, None], sin[:, :, None]
    q = apply_rope(q.reshape(b, s, hq, dh), cos, sin)
    q = q.reshape(b, s, g_, hpg, dh).transpose(0, 2, 3, 1, 4)

    def kv_heads(t):
        return t.reshape(b, s, g_, dh)

    k_s = apply_rope(kv_heads(k_s), cos, sin).transpose(0, 2, 1, 3)
    v_s = kv_heads(v_s).transpose(0, 2, 1, 3)
    k_w = apply_rope(kv_heads(k_w), cos, sin).transpose(0, 2, 1, 3)
    v_w = kv_heads(v_w).transpose(0, 2, 1, 3)
    k_cmp = compress_blocks(kv_heads(k_c), cmp_pos_k, cmp_w1_k, cmp_w2_k)
    v_cmp = compress_blocks(kv_heads(v_c), cmp_pos_v, cmp_w1_v, cmp_w2_v)
    n_cmp = k_cmp.shape[2]
    cmp_end = jnp.arange(n_cmp) * CMP_STRIDE + CMP_BLOCK - 1
    ccos, csin = rope_angles(positions[:, cmp_end])
    k_cmp = apply_rope(k_cmp, ccos[:, None], csin[:, None])
    valid_c = cmp_end[None, :] <= jnp.arange(s)[:, None]
    sc = jnp.einsum('bghsd,bgnd->bghsn', q, k_cmp).astype(jnp.float32) * ATTN_SCALE
    p_cmp = jax.nn.softmax(jnp.where(valid_c, sc, NEG_INF), axis=-1) * valid_c
    o_cmp = jnp.einsum('bghsn,bgnd->bghsd', p_cmp.astype(v_cmp.dtype), v_cmp)
    idx = select_blocks(jnp.sum(p_cmp, axis=2), s)
    o_slc = selected_attention(q, k_s, v_s, idx)
    o_win = window_attention(q, k_w, v_w)
    gt = jax.nn.sigmoid(gates.astype(jnp.float32)).reshape(b, s, g_, hpg, 3)
    gt = gt.transpose(0, 2, 3, 1, 4).astype(x.dtype)
    o = gt[..., 0:1] * o_cmp + gt[..., 1:2] * o_slc + gt[..., 2:3] * o_win
    o = o.transpose(0, 3, 1, 2, 4).reshape(b, s, hq * dh)
    return o @ w_out

def swiglu_ffn(x, w_in, w_out):
    gate, up = jnp.split(x @ w_in, 2, axis=-1)
    return (jax.nn.silu(gate) * up) @ w_out

def setup_inputs(seed: int = 0) -> dict:
    key = jax.random.key(seed)
    ks = jax.random.split(key, 24)
    f32 = jnp.float32

    def nrm(k, shape, fan_in, gain=1.0):
        return jax.random.normal(k, shape, f32) * (gain * fan_in ** -0.5)

    x = jax.random.normal(ks[0], (BATCH, SEQ, D_MODEL), f32)
    offset = jax.random.randint(ks[1], (BATCH, 1), 0, 4096, dtype=jnp.int32)
    positions = offset + jnp.arange(SEQ, dtype=jnp.int32)[None, :]
    ln_mix_g = 1.0 + 0.02 * jax.random.normal(ks[2], (DEPTH, D_MODEL), f32)
    ln_mix_b = 0.02 * jax.random.normal(ks[3], (DEPTH, D_MODEL), f32)
    ln_ffn_g = 1.0 + 0.02 * jax.random.normal(ks[4], (DEPTH, D_MODEL), f32)
    ln_ffn_b = 0.02 * jax.random.normal(ks[5], (DEPTH, D_MODEL), f32)
    ffn_w_in = nrm(ks[6], (DEPTH, D_MODEL, 2 * FFN_HIDDEN), D_MODEL)
    ffn_w_out = nrm(ks[7], (DEPTH, FFN_HIDDEN, D_MODEL), FFN_HIDDEN, DEEPNORM_BETA)
    hy_w_in = nrm(ks[8], (N_EVEN, D_MODEL, HY_COLS), D_MODEL)
    sc_conv_w = nrm(ks[9], (N_EVEN, SC_KERNEL, SC_WIDTH), SC_KERNEL)
    dn_conv_w = nrm(ks[10], (N_EVEN, DN_CONV, 3 * DN_WIDTH), DN_CONV)
    dn_a_log = jnp.log(jax.random.uniform(ks[11], (N_EVEN, DN_HEADS), f32, 1.0, 16.0))
    dt = jnp.exp(jax.random.uniform(ks[12], (N_EVEN, DN_HEADS), f32, math.log(1e-3), math.log(1e-1)))
    dn_dt_bias = dt + jnp.log(-jnp.expm1(-dt))
    dn_norm_w = 1.0 + 0.02 * jax.random.normal(ks[13], (N_EVEN, DN_HEAD_DIM), f32)
    hy_w_out = nrm(ks[14], (N_EVEN, D_MODEL, D_MODEL), D_MODEL, DEEPNORM_BETA)
    nsa_w_in = nrm(ks[15], (N_ODD, D_MODEL, NSA_COLS), D_MODEL)
    cmp_pos_k = 0.1 * jax.random.normal(ks[16], (N_ODD, CMP_BLOCK, NSA_HEAD_DIM), f32)
    cmp_w1_k = nrm(ks[17], (N_ODD, CMP_BLOCK * NSA_HEAD_DIM, CMP_HIDDEN), CMP_BLOCK * NSA_HEAD_DIM)
    cmp_w2_k = nrm(ks[18], (N_ODD, CMP_HIDDEN, NSA_HEAD_DIM), CMP_HIDDEN)
    cmp_pos_v = 0.1 * jax.random.normal(ks[19], (N_ODD, CMP_BLOCK, NSA_HEAD_DIM), f32)
    cmp_w1_v = nrm(ks[20], (N_ODD, CMP_BLOCK * NSA_HEAD_DIM, CMP_HIDDEN), CMP_BLOCK * NSA_HEAD_DIM)
    cmp_w2_v = nrm(ks[21], (N_ODD, CMP_HIDDEN, NSA_HEAD_DIM), CMP_HIDDEN)
    nsa_w_out = nrm(ks[22], (N_ODD, D_MODEL, D_MODEL), D_MODEL, DEEPNORM_BETA)
    return {'x': x, 'positions': positions,
            'ln_mix_g': ln_mix_g, 'ln_mix_b': ln_mix_b, 'ln_ffn_g': ln_ffn_g, 'ln_ffn_b': ln_ffn_b,
            'ffn_w_in': ffn_w_in, 'ffn_w_out': ffn_w_out,
            'hy_w_in': hy_w_in, 'sc_conv_w': sc_conv_w, 'dn_conv_w': dn_conv_w,
            'dn_a_log': dn_a_log, 'dn_dt_bias': dn_dt_bias, 'dn_norm_w': dn_norm_w, 'hy_w_out': hy_w_out,
            'nsa_w_in': nsa_w_in, 'cmp_pos_k': cmp_pos_k, 'cmp_w1_k': cmp_w1_k, 'cmp_w2_k': cmp_w2_k,
            'cmp_pos_v': cmp_pos_v, 'cmp_w1_v': cmp_w1_v, 'cmp_w2_v': cmp_w2_v, 'nsa_w_out': nsa_w_out}

def reference(x, positions, ln_mix_g, ln_mix_b, ln_ffn_g, ln_ffn_b, ffn_w_in, ffn_w_out,
              hy_w_in, sc_conv_w, dn_conv_w, dn_a_log, dn_dt_bias, dn_norm_w, hy_w_out,
              nsa_w_in, cmp_pos_k, cmp_w1_k, cmp_w2_k, cmp_pos_v, cmp_w1_v, cmp_w2_v, nsa_w_out):
    for i in range(DEPTH):
        j = i // 2
        if i % 2 == 0:
            y = conv_deltanet_mixer(x, hy_w_in[j], sc_conv_w[j], dn_conv_w[j], dn_a_log[j],
                                    dn_dt_bias[j], dn_norm_w[j], hy_w_out[j])
        else:
            y = nsa_mixer(x, positions, nsa_w_in[j], cmp_pos_k[j], cmp_w1_k[j], cmp_w2_k[j],
                          cmp_pos_v[j], cmp_w1_v[j], cmp_w2_v[j], nsa_w_out[j])
        x = layer_norm(DEEPNORM_ALPHA * x + y, ln_mix_g[i], ln_mix_b[i])
        x = layer_norm(DEEPNORM_ALPHA * x + swiglu_ffn(x, ffn_w_in[i], ffn_w_out[i]), ln_ffn_g[i], ln_ffn_b[i])
    return x


_drawn_inputs = setup_inputs


def setup_inputs(seed=0):
    import zlib

    import numpy as np

    out = dict(_drawn_inputs(seed))
    spreads = {}
    factors = {'dn_norm_w': 74.313, 'cmp_pos_k': 8.0, 'cmp_w1_k': 2.706, 'cmp_pos_v': 4.93}
    for name, (base, spread) in spreads.items():
        noise = np.random.default_rng([zlib.crc32(name.encode()), seed]).standard_normal(out[name].shape)
        drawn = base * np.exp(spread * noise) if base else spread * noise
        out[name] = jnp.asarray(drawn.astype(out[name].dtype))
    for name, factor in factors.items():
        out[name] = (out[name] * factor).astype(out[name].dtype)
    return out
```

```python
from contextlib import ExitStack

import numpy as np
import concourse.bass as bass
from concourse import mybir

F32 = mybir.dt.float32
F32R = mybir.dt.float32r
I32 = mybir.dt.int32
ALU = mybir.AluOpType
ACT = mybir.ActivationFunctionType
AX = mybir.AxisListType
ds = bass.ds

P = 128
D = 2048
KT = D // P
SEQ = 256
NT = SEQ // P
DEPTH = 2
FFN = ((8 * D + 3 * 256 - 1) // (3 * 256)) * 256
FT = FFN // P
CH = 512
SC = D // 2
SCK, DNK = 3, 4
DNH = 8
NH, NG = 16, 4
HPG = NH // NG
DH = 128
CMPB, STRIDE = 32, 16
NCMP = SEQ // STRIDE - CMPB // STRIDE + 1
NCG = NCMP * NG
CMPH = 2 * DH
ALPHA = (2 * DEPTH) ** 0.25
LN_EPS, NORM_EPS = 1e-5, 1e-6
NEG = -1e30
SCALE = DH ** -0.5
TWO_PI_1 = 6.28125
TWO_PI_2 = float(np.float32(2 * np.pi - 6.28125))
TWO_PI_3 = float(2 * np.pi - 6.28125 - TWO_PI_2)
PI = 3.1415925
ROUND = 1.5 * 2.0 ** 23

RAW_SLOTS, HL_SLOTS = 4, 4
STOP = None
BLOCKS = (1, 2, 4, 8, 16, 32, 64)


def at(c, i=None, per=0):
    return c if i is None else i * per + c


class Plan:

    def __init__(self):
        self.slab, self.chunk = {}, {}
        s = c = 0
        for name, slabs, chunks in (
            ("ba", 1, 1), ("z", 8, 2), ("qkv", 24, 6), ("sc", 24, 6), ("out0", 16, 0),
            ("ffn0", 88, 22), ("fout0", FT, 0),
            ("gates", 1, 1), ("kcvc", 8, 2), ("w1", 8, 2), ("kv", 16, 4), ("q", 16, 4), ("out1", 16, 0),
            ("ffn1", 88, 22), ("fout1", FT, 0),
        ):
            self.slab[name], self.chunk[name] = s, c
            s, c = s + slabs, c + chunks


def trunk(nc, x_in, positions, ln_mix_g, ln_mix_b, ln_ffn_g, ln_ffn_b, ffn_w_in, ffn_w_out,
          hy_w_in, sc_conv_w, dn_conv_w, dn_a_log, dn_dt_bias, dn_norm_w, hy_w_out,
          nsa_w_in, cmp_pos_k, cmp_w1_k, cmp_w2_k, cmp_pos_v, cmp_w1_v, cmp_w2_v, nsa_w_out,
          inv_freq, ln_by_feature, end_positions, out, stop=None):
    plan = Plan()
    S, C = plan.slab, plan.chunk
    ctx = ExitStack()
    with ctx:
        def sem(name):
            return ctx.enter_context(nc.semaphore(name))

        place = [16512]

        def sb(name, shape, dt=F32, offset=None):
            size = 4 * int(np.prod(shape[1:]))
            if offset is None:
                offset = place[0]
                place[0] += (size + 31) // 32 * 32
            return nc.alloc_sbuf_tensor_at(name, shape, dt, offset=offset)

        raw = sb("raw", [P, RAW_SLOTS, 2048])
        w_hi = sb("w_hi", [P, HL_SLOTS, 1024], F32R)
        w_lo = sb("w_lo", [P, HL_SLOTS, 1024], F32R)
        xt_hi = sb("xt_hi", [P, KT, SEQ], F32R)
        xt_lo = sb("xt_lo", [P, KT, SEQ], F32R)
        x = sb("x", [P, NT, D])
        a_hi = sb("a_hi", [P, 4, SEQ], F32R)
        a_lo = sb("a_lo", [P, 4, SEQ], F32R)
        big = sb("big", [P, 12288])
        yt = sb("yt", [P, KT, SEQ])
        gb_at = place[0]
        gb = sb("gb", [P, 2, D])
        ident = sb("ident", [P, P])
        ones = sb("ones", [P, P])
        upper = sb("upper", [P, P])
        neg_lower = sb("neg_lower", [P, P])
        blk_mask = sb("blk_mask", [P, len(BLOCKS), P])
        lnT = sb("lnT", [P, 2, KT])
        stats = sb("stats", [P, NT, 4, 6])
        mv = sb("mv", [P, NT, 2])
        rstd = sb("rstd", [P, NT])
        nmr = sb("nmr", [P, NT])
        eps_ln = sb("eps_ln", [P, 1])
        eps_nm = sb("eps_nm", [P, 1])
        half_pi = sb("half_pi", [P, 1])
        sm = sb("sm", [P, 16, 16])
        misc_w = sb("misc_w", [P, 136])

        used = 0

        def part(n, shape_str=None, **kw):
            nonlocal used
            v = big[:, used:used + n]
            used += n
            assert used <= 12288
            return v.rearrange(shape_str, **kw) if shape_str else v

        qkvT = part(24 * SEQ, "p (f t) -> p f t", f=24)
        k_tok = part(1024, "p (h d) -> p h d", h=DNH)
        state = part(1024, "p (h d) -> p h d", h=DNH)
        norm_w = state[:, 0, :]
        v_tok = part(2048, "p (t h d) -> p t h d", t=NT, h=DNH)
        z_tok = part(2048, "p (t h d) -> p t h d", t=NT, h=DNH)
        vT = qkvT[:, 16:24, :]
        vT_flat = big[:, 16 * SEQ:24 * SEQ]
        gb_flat = gb[:, :, :].rearrange("p a n -> p (a n)")

        def dn_tile(n):
            base, m = (gb_flat, n) if n < 8 else (vT_flat, n - 8)
            return base[:, m * 512:(m + 1) * 512].rearrange("p (h d) -> p h d", h=4)
        conv_in = gb_flat[:, 0:2048].rearrange("p (a f t) -> p a f t", a=2, f=4)
        conv_out = gb_flat[:, 2048:3072].rearrange("p (f t) -> p f t", f=4)
        hT = big[:, 0:FT * SEQ].rearrange("p (f t) -> p f t", f=FT)
        yt_flat = yt[:, :, :].rearrange("p a t -> p (a t)")
        sg = yt_flat[:, 0:1024].rearrange("p (t n) -> p t n", t=NT)
        hid = yt_flat[:, 1024:2048].rearrange("p (t n) -> p t n", t=NT)
        used = 0
        qT = part(NH * SEQ, "p (h t) -> p h t", h=NH)
        ksT = part(2 * NG * SEQ, "p (b h t) -> p b h t", b=2, h=NG)
        vs = part(2 * NT * 512, "p (b t n) -> p b t n", b=2, t=NT)
        kcT = part(2 * NG * SEQ, "p (b h t) -> p b h t", b=2, h=NG)
        kcmpT = part(64)
        vcmp = part(NG * DH, "p (g d) -> p g d", g=NG)
        w2 = part(2 * 2 * DH, "p (b k n) -> p b k n", b=2, k=2)
        neg_cmp = part(NT * NCMP, "p (t n) -> p t n", t=NT)
        ok_cmp = part(NT * NCMP, "p (t n) -> p t n", t=NT)
        cmp_hT = part(128, "p (k n) -> p k n", k=2)
        neg_upper = part(2 * P, "p (a n) -> p a n", a=2)
        posT = part(2 * CMPB, "p (b l) -> p b l", b=2)
        rope_in = yt_flat[:, 0:1024].rearrange("p (t n) -> p t n", t=NT)
        rope_a = yt_flat[:, 1024:2048].rearrange("p (t n) -> p t n", t=NT)
        rope_b = yt_flat[:, 2048:3072].rearrange("p (t n) -> p t n", t=NT)
        cosb = yt_flat[:, 3072:3328].rearrange("p (t n) -> p t n", t=NT)
        sinb = yt_flat[:, 3328:3584].rearrange("p (t n) -> p t n", t=NT)
        cosc = yt_flat[:, 3584:3712]
        sinc = yt_flat[:, 3712:3840]
        blk_sum = yt_flat[:, 0:CMPB * NCG].rearrange("p (l r) -> p l r", l=CMPB)
        angle = yt_flat[:, 2048:2240].rearrange("p (a n) -> p a n", a=3)
        turns = yt_flat[:, 2240:2432].rearrange("p (a n) -> p a n", a=3)
        sc_buf = [gb_flat[:, 1024 * n:1024 * n + 1024] for n in range(2)]
        pT_buf = [gb_flat[:, 2048 + 1024 * n:3072 + 1024 * n].rearrange("p (k m) -> p k m", k=2) for n in range(2)]
        kc_flat = kcT.rearrange("p b h t -> p (b h t)")
        o_buf = kc_flat[:, 0:512].rearrange("p (h d) -> p h d", h=HPG)
        sc_cmp = kc_flat[:, 512:512 + HPG * NCMP].rearrange("p (h n) -> p h n", h=HPG)
        pT_cmp = kc_flat[:, 640:1152]
        gates = sm[:, 8:14, :].rearrange("p a b -> p (a b)").rearrange("p (t n) -> p t n", t=NT)
        blk_hi = sb("blk_hi", [P, CMPB, NCG], F32R, offset=gb_at)
        blk_lo = sb("blk_lo", [P, CMPB, NCG], F32R, offset=gb_at + 4 * CMPB * NCG)

        bank = [ctx.enter_context(nc.psum_tensor(f"bank{n}", [P, 512], F32)) for n in range(8)]

        def pair(c):
            return bank[2 * (c % 2)], bank[2 * (c % 2) + 1]

        slab_in = [sem(f"slab_in{n}") for n in range(RAW_SLOTS)]
        w_hi_ready, w_lo_ready = sem("w_hi_ready"), sem("w_lo_ready")
        half_used = sem("half_used")
        a_hi_ready, a_lo_ready = sem("a_hi_ready"), sem("a_lo_ready")
        pair_free = [sem(f"pair_free{n}") for n in range(2)]
        sp_ready = [sem(f"sp_ready{n}") for n in range(4)]
        sp_free = [sem(f"sp_free{n}") for n in range(4)]
        x_in_sem, small_in, nsa_in = sem("x_in_sem"), sem("small_in"), sem("nsa_in")
        gb_in, out_done = sem("gb_in"), sem("out_done")
        consts, pool_chain, x_scaled = sem("consts"), sem("pool_chain"), sem("x_scaled")
        dve, act_done = sem("dve"), sem("act_done")
        var_ready, std_ready, nmr_ready, x_normed = sem("var_ready"), sem("std_ready"), sem("nmr_ready"), sem("x_normed")
        xt_hi_ready, xt_lo_ready = sem("xt_hi_ready"), sem("xt_lo_ready")
        stage_free, silu_done = sem("stage_free"), sem("silu_done")
        hid_ready = sem("hid_ready")
        first_whole = sem("first_whole")
        ident_ready, out_ready = sem("ident_ready"), sem("out_ready")
        for_act, for_pe, from_act, gb_free = sem("for_act"), sem("for_pe"), sem("from_act"), sem("gb_free")

        block = ctx.enter_context(nc.Block())

        def pair(c):
            return bank[2 * (c % 2)], bank[2 * (c % 2) + 1]

        K, n_uses = {}, 0

        def uses(names):
            nonlocal n_uses
            for name in names:
                K[name] = n_uses
                n_uses += 1

        uses([("xT", 0, u) for u in range(8)])
        uses([("gc",)])
        uses([("norm", u) for u in range(8)])
        uses([("ktok", hh) for hh in range(2)] + [("vtok", t, hh) for t in range(NT) for hh in range(2)])
        for t in range(NT):
            for hh in range(2):
                uses([("row", t, hh), ("beta", t, hh), ("kk", t, hh), ("kq", t, hh)])
            uses([("eT", t, hh) for hh in range(2)])
            for n in range(1, len(BLOCKS)):
                uses([("g", t, n, hh) for hh in range(2)])
                for hh in range(2):
                    uses([("x", t, n, hh)] + [("t", t, n, hh)] * (n < len(BLOCKS) - 1))
            if t:
                for hh in range(2):
                    uses([("ks", hh), ("qs", hh)])
            uses([("v", t, hh) for hh in range(2)])
            for hh in range(2):
                uses([("o", t, hh)] + [("s", hh)] * (t == 0))
            uses([("y", t, hh) for hh in range(2)])
        uses([("xT", 1, u) for u in range(8)])
        uses([("ffn", 0, n) for n in range(2 * FFN // CH)])
        uses([("xT", 2, u) for u in range(8)])
        uses([("kcmp",), ("vcmp",), ("kcmpT",)])
        uses([("kv", b, a) for b in range(2) for a in range(2)])
        uses([("q", n) for n in range(8)])
        for g in range(NG):
            for t in range(NT):
                uses([("c", g, t)] + [("s", g, t, b, k) for b in range(2) for k in range(t + 1)])
                uses([("cT", g, t)] + [("pT", g, t, b, k) for b in range(2) for k in range(t + 1)])
                uses([("co", g, t)] + [("po", g, t, b) for b in range(2)] + [("oT", g, t)])
        uses([("xT", 3, u) for u in range(8)])
        uses([("ffn", 1, n) for n in range(2 * FFN // CH)])

        def sp_bank(name):
            return bank[4 + K[name] % 4]

        def wait_sp(eng, name, i=None, per=0):
            eng.wait_ge(sp_ready[K[name] % 4], at(K[name] // 4 + 1, i, per // 4))

        def wait_sp_read(eng, name):
            eng.wait_ge(sp_free[K[name] % 4], K[name] // 4 + 1)

        chunk_end = {}
        for name, m in (("ba", 0), ("z", 2), ("qkv", 6), ("sc", 6), ("ffn0", 22), ("gates", 0), ("kcvc", 2), ("w1", 2),
                        ("kv", 4), ("q", 4), ("ffn1", 22)):
            for n in range(m or 1):
                chunk_end[C[name] + n] = 2 * S[name] + (8 * (n + 1) if m else 2)

        FP, n_fp = {}, 0

        def hands(names):
            nonlocal n_fp
            for name in names:
                n_fp += 1
                FP[name] = n_fp

        hands([("g",)] + [("kn",)])
        for t in range(NT):
            hands([("rows", t, hh) for hh in range(2)])
            hands([("m", t, 0, hh) for hh in range(2)])
            for n in range(1, len(BLOCKS)):
                hands([("m", t, n, hh) for hh in range(2)])
            hands([("rhs", t, hh) for hh in range(2)])
            hands([("on", t, hh) for hh in range(2)])

        @block.sync
        def _(sp):
            def slab(s, src, view, i=None, per=0):
                if s >= RAW_SLOTS:
                    sp.wait_ge(w_lo_ready, at(2 * (s - RAW_SLOTS) + 2, i, 2 * per))
                sp.dma_start(view(raw[:, s % RAW_SLOTS, :]), src).then_inc(slab_in[s % RAW_SLOTS], 16)

            def as_in(v):
                return v.rearrange("p (k n) -> p k n", k=4)

            def cols(w, quad, col):
                return w[quad * 512:(quad + 1) * 512, col].rearrange("(k p) n -> p k n", p=P)

            def small(name, w, lo, n):
                slab(S[name], w[:, lo:lo + n].rearrange("(k p) n -> p k n", p=P),
                     lambda v: v[:, 0:KT * n].rearrange("p (k n) -> p k n", k=KT))

            def chunk(s, w, col, i=None, per=0):
                for quad in range(4):
                    slab(s + quad, cols(w, quad, col), as_in, i, per)

            def outer(name, w, n):
                with sp.Fori(0, n // 4) as i:
                    for j in range(4):
                        slab(S[name] + j, w[ds(i * 512 + j * P, P), :], lambda v: v, i, 4)

            def ffn(name, layer):
                w = ffn_w_in[layer]
                for j in range(2):
                    chunk(S[name] + 4 * j, w, slice(j * FFN, j * FFN + CH))
                with sp.Fori(0, 5) as i:
                    for n in range(4):
                        chunk(S[name] + 8 + 4 * n, w, ds(i * 2 * CH + (n // 2 + 1) * CH + (n % 2) * FFN, CH), i, 16)
                outer("fout" + name[-1], ffn_w_out[layer], FT)

            for t in range(NT):
                sp.dma_start(x[:, t, :], x_in[0, t * P:(t + 1) * P, :]).then_inc(x_in_sem, 16)
            w = hy_w_in[0]
            small("ba", w, 7168, 16)
            for j in range(2):
                chunk(S["z"] + 4 * j, w, slice(6144 + j * CH, 6144 + (j + 1) * CH))
            with sp.Fori(0, 3) as i:
                for j in range(2):
                    chunk(S["qkv"] + 4 * j, w, ds(i * 2 * CH + 3 * SC + j * CH, CH), i, 8)
            for j in range(2):
                for n, lo in enumerate((SC, 2 * SC, 0)):
                    chunk(S["sc"] + 12 * j + 4 * n, w, slice(lo + j * CH, lo + (j + 1) * CH))
            outer("out0", hy_w_out[0], KT)
            ffn("ffn0", 0)
            if stop != "l0":
                w = nsa_w_in[0]
                small("gates", w, 5120, 48)
                for b in range(2):
                    chunk(S["kcvc"] + 4 * b, w, slice(2048 + b * CH, 2048 + (b + 1) * CH))
                for b, w1 in enumerate((cmp_w1_k, cmp_w1_v)):
                    for q in range(4):
                        slab(S["w1"] + 4 * b + q, w1[0][q * 1024:(q + 1) * 1024, :].rearrange("(l p) n -> p l n", p=P),
                             lambda v: v.rearrange("p (l n) -> p l n", l=8))
                for n in range(4):
                    chunk(S["kv"] + 4 * n, w, slice(3072 + n * CH, 3072 + (n + 1) * CH))
                for j in range(4):
                    chunk(S["q"] + 4 * j, w, slice(j * CH, (j + 1) * CH))
                outer("out1", nsa_w_out[0], KT)
                ffn("ffn1", 1)
            for n in range(2 * NT):
                sp.wait_ge(out_ready, n + 1)
                rows, col = slice(n // 2 * P, (n // 2 + 1) * P), slice(n % 2 * D // 2, (n % 2 + 1) * D // 2)
                sp.dma_start(out[0, rows, col], x[:, n // 2, col]).then_inc(out_done, 16)
            sp.wait_ge(out_done, 16 * 2 * NT)

        @block.gpsimd
        def _(pool):
            def bcast(ap, n):
                return ap.rearrange("(a n) -> a n", a=1).to_broadcast([P, n])

            count = [0]

            def own(ins):
                count[0] += 1
                ins.then_inc(pool_chain, 1)
                pool.wait_ge(pool_chain, count[0])

            def select(ap, pattern, base, mult, fill):
                own(pool.affine_select(out=ap, in_=ap, pattern=pattern, compare_op=ALU.is_ge, fill=fill,
                                       base=base, channel_multiplier=mult))

            own(pool.memset(ident[:, :], 0.0))
            pool.affine_select(out=ident[:, :], in_=ident[:, :], pattern=[[-1, P]], compare_op=ALU.not_equal, fill=1.0,
                               base=0, channel_multiplier=1).then_inc(ident_ready, 1)
            for m, v in ((ones, 1.0), (upper, 1.0), (neg_lower, 0.0), (blk_mask, 0.0)):
                own(pool.memset(m[:, :] if len(m.shape) == 2 else m[:, :, :], v))
            select(upper[:, :], [[1, P]], 0, -1, 0.0)
            select(neg_lower[:, :], [[1, P]], 0, -1, NEG)
            for n, b in enumerate(BLOCKS):
                v = blk_mask[:, n, :].rearrange("p (m a r) -> p m a r", a=2, r=b)[:, :, 1, :]
                own(pool.memset(v, 1.0))
                select(v, [[-2 * b, P // (2 * b)], [0, b]], 0, 1, 0.0)
                select(v, [[2 * b, P // (2 * b)], [0, b]], b - 1, -1, 0.0)
            pool.memset(eps_ln[:, :], LN_EPS).then_inc(consts, 1)
            pool.memset(eps_nm[:, :], NORM_EPS).then_inc(consts, 1)
            pool.memset(half_pi[:, :], float(np.pi / 2)).then_inc(consts, 1)
            pool.dma_start(misc_w[:, 0:96], dn_conv_w).then_inc(small_in, 16)
            pool.dma_start(misc_w[:, 96:120], sc_conv_w).then_inc(small_in, 16)
            pool.dma_start(norm_w, bcast(dn_norm_w[0], DH)).then_inc(small_in, 16)
            pool.dma_start(misc_w[:, 120:128], bcast(dn_a_log[0], DNH)).then_inc(small_in, 16)
            pool.dma_start(misc_w[:, 128:136], bcast(dn_dt_bias[0], DNH)).then_inc(small_in, 16)

            def layer_norm(n, g, b):
                pool.wait_ge(gb_free, n + 1)
                if n:
                    pool.wait_ge(x_scaled, NT * n)
                for a, v in enumerate((g, b)):
                    pool.dma_start(gb[:, a, :], bcast(v, D)).then_inc(gb_in, 16)
                pool.dma_start(lnT[:, :, :], ln_by_feature[:, n, :, :]).then_inc(gb_in, 16)
                pool.wait_ge(gb_in, 48 * (n + 1))
                last = 2 * DEPTH - 1 if stop != "l0" else 1
                if n < last:
                    for bk in range(4):
                        wait_sp(pool, ("xT", n + 1, 4 + bk))
                else:
                    return
                for t in range(NT):
                    own(pool.tensor_tensor(x[:, t, :], x[:, t, :], gb[:, 0, :], ALU.mult))
                    pool.tensor_tensor(x[:, t, :], x[:, t, :], gb[:, 1, :], ALU.add).then_inc(x_scaled, 1)

            layer_norm(0, ln_mix_g[0], ln_mix_b[0])
            layer_norm(1, ln_ffn_g[0], ln_ffn_b[0])
            if stop != "l0":
                for t in range(NT):
                    for m, v, fill in ((neg_cmp, 0.0, NEG), (ok_cmp, 1.0, 0.0)):
                        own(pool.memset(m[:, t, :], v))
                        select(m[:, t, :], [[-STRIDE, NCMP]], t * P - (CMPB - 1), 1, fill)
                own(pool.memset(neg_upper, 0.0))
                select(neg_upper[:, 1, :], [[-1, P]], 0, 1, NEG)
                pool.wait_ge(xt_lo_ready, 12)
                for t in range(NT):
                    pool.dma_start(angle[:, t, 0:1].bitcast(I32), positions[0][t * P:(t + 1) * P].rearrange("(p a) -> p a", a=1)).then_inc(nsa_in, 16)
                pool.dma_start(angle[0:NCG, 2, 0:1].bitcast(I32), end_positions).then_inc(nsa_in, 16)
                for a in range(3):
                    pool.dma_start(turns[:, a, :], bcast(inv_freq, DH // 2)).then_inc(nsa_in, 16)
                for b, (w, p) in enumerate(((cmp_w2_k, cmp_pos_k), (cmp_w2_v, cmp_pos_v))):
                    pool.dma_start(w2[:, b, :, :], w[0].rearrange("(k p) n -> p k n", p=P)).then_inc(nsa_in, 16)
                    pool.dma_start(posT[:, b, :], p).then_inc(nsa_in, 16)
                layer_norm(2, ln_mix_g[1], ln_mix_b[1])
                layer_norm(3, ln_ffn_g[1], ln_ffn_b[1])

        total_slabs = S["gates"] if stop == "l0" else S["fout1"] + FT
        small_n = {2 * S["ba"] + n: KT // 2 * 16 for n in range(2)}
        small_n.update({2 * S["gates"] + n: KT // 2 * 48 for n in range(2)})
        LEAD = 3
        A0 = {"out0": 0, "fout0": KT, "out1": KT + FT, "fout1": 2 * KT + FT}

        def half_of(h):
            n = small_n.get(h, 1024)
            return raw[:, h // 2 % RAW_SLOTS, h % 2 * n:h % 2 * n + n], h % HL_SLOTS, n

        def outer_src(name):
            return hT if name[0] == "f" else yt

        @block.scalar
        def _(act):
            h_next = [0]

            def halves(count, i=None, per=0):
                for _ in range(count):
                    h = h_next[0]
                    if h >= 2 * total_slabs:
                        return
                    src, slot, n = half_of(h)
                    if h % 2 == 0:
                        act.wait_ge(slab_in[h // 2 % RAW_SLOTS], at(16 * (h // 2 // RAW_SLOTS + 1), i, 2 * per))
                    if h >= HL_SLOTS:
                        act.wait_ge(half_used, at(h - HL_SLOTS + 1, i, per))
                    act.activation(w_hi[:, slot, 0:n], src, ACT.Copy).then_inc(w_hi_ready, 1)
                    h_next[0] += 1

            def loop_over(n, per_halves, body):
                with act.Fori(0, n) as i:
                    body(i)
                h_next[0] += (n - 1) * per_halves

            def chunk_in(c, i=None, per=0):
                act.wait_ge(half_used, at(chunk_end[c], i, 16 * per))
                return pair(c)

            def split_xt(m):
                for q in range(4):
                    for u in (2 * q, 2 * q + 1):
                        wait_sp_read(act, ("xT", m, u))
                    act.activation(xt_hi[:, 4 * q:4 * q + 4, :], yt[:, 4 * q:4 * q + 4, :], ACT.Copy).then_inc(xt_hi_ready, 1)

            def outer(name, n):
                src = outer_src(name)

                def split(kt, i=None):
                    act.wait_ge(half_used, at(2 * (S[name] + kt) - 6, i, 8))
                    col = kt if i is None else ds(i * 4 + kt, 1)
                    s_ = src[:, col, :]
                    act.activation(a_hi[:, kt % 4, :], s_, ACT.Copy).then_inc(a_hi_ready, 1)

                def quad(kt, i=None):
                    for j in range(4):
                        if kt + j + 1 < n:
                            split(kt + j + 1, i)
                        halves(2, i, 8)
                split(0)
                loop_over(n // 4 - 1, 8, lambda i: quad(0, i))
                quad(n - 4)

            def ln(n, last=False):
                def normalise(t):
                    act.wait_ge(nmr_ready, NT * n + t + 1)
                    m = 4 if t else 1
                    for c in range(m):
                        v = x[:, t, c * D // m:(c + 1) * D // m]
                        act.activation(v, v, ACT.Identity, bias=nmr[:, t:t + 1], scale=rstd[:, t:t + 1]).then_inc(x_normed, 1)

                for t in range(NT):
                    act.wait_ge(var_ready, NT * n + t + 1)
                    act.activation(rstd[:, t:t + 1], mv[:, t, 1:2], ACT.Sqrt, bias=eps_ln[:, :]).then_inc(std_ready, 1)
                    if t == 0 and not last:
                        normalise(0)
                if not last:
                    normalise(1)

            def ffn(layer):
                c0, k0 = C[f"ffn{layer}"], K[("ffn", layer, 0)]
                n_sg = layer * (FFN // CH)

                def gate(c, n, i=None):
                    b = chunk_in(c, i, 2)
                    if n_sg + n > 0:
                        act.wait_ge(hid_ready, at(n_sg + n, i, 2))
                    for t in range(NT):
                        ins = act.activation(sg[:, t, :], b[t][:, :], ACT.Silu)
                    ins.then_inc(pair_free[c % 2], 1)

                def put_hT(k, f, i=None):
                    for a in range(2):
                        act.wait_ge(sp_ready[(k + a) % 4], at((k + a) // 4 + 1, i, 1))
                        col = slice(f + 2 * a, f + 2 * a + 2) if i is None else ds(i * 8 + f + 2 * a, 2)
                        dst = hT[:, col, :]
                        act.activation(dst, bank[4 + (k + a) % 4][:, :].rearrange("p (a t) -> p a t", a=2),
                                       ACT.Copy).then_inc(sp_free[(k + a) % 4], 1)

                halves(8)
                gate(c0, 0)
                halves(8)

                def body(i):
                    for n in range(2):
                        halves(8, i, 32)
                        gate(c0 + 2 + 2 * n, 1 + n, i)
                        put_hT(k0 + 2 * n, 4 * n, i)
                        halves(8, i, 32)
                loop_over(5, 32, body)
                put_hT(k0 + 20, 40)
                for a in range(2):
                    act.wait_ge(sp_free[(k0 + 20 + a) % 4], (k0 + 20 + a) // 4 + 1)
                outer(f"fout{layer}", FT)

            halves(LEAD)
            split_xt(0)
            halves(2)
            b = chunk_in(C["ba"])
            for t in range(NT):
                ins = act.activation(sm[:, t, :], b[t][:, 0:16], ACT.Copy)
            ins.then_inc(pair_free[0], 1)
            for j in range(2):
                halves(8)
                c = C["z"] + j
                b = chunk_in(c)
                for t in range(NT):
                    ins = act.activation(z_tok[:, t, 4 * j:4 * j + 4, :], b[t][:, :].rearrange("p (h d) -> p h d", h=4), ACT.Silu)
                ins.then_inc(pair_free[c % 2], 1)

            def qkv_turn(i):
                for j in range(2):
                    halves(8, i, 16)
                    c = C["qkv"] + j
                    b = chunk_in(c, i, 1)
                    act.wait_ge(stage_free, at(j + 1, i, 2))
                    for n in range(2):
                        ins = act.activation(conv_in[:, j, 2 * n:2 * n + 2, :],
                                             b[n][:, :].rearrange("p (f t) -> p f t", f=2), ACT.Copy)
                    ins.then_inc(pair_free[c % 2], 1)
            loop_over(3, 16, qkv_turn)
            for j in range(2):
                for n in range(3):
                    halves(8)
                    if n == 0:
                        c = C["sc"] + 3 * j
                        b = chunk_in(c)
                        act.wait_ge(stage_free, 7 + j)
                        for a in range(2):
                            ins = act.activation(conv_in[:, j, 2 * a:2 * a + 2, :],
                                                 b[a][:, :].rearrange("p (f t) -> p f t", f=2), ACT.Copy)
                        ins.then_inc(pair_free[c % 2], 1)
                    m = 3 * j + n
                    act.wait_ge(stage_free, m + 3)
                    act.activation(qkvT[:, 4 * m:4 * m + 4, :], qkvT[:, 4 * m:4 * m + 4, :], ACT.Silu).then_inc(silu_done, 1)

            act.wait_ge(consts, 3)
            n_from = [0]

            def done(ins):
                n_from[0] += 1
                ins.then_inc(from_act, 1)

            soft, expA = sm[:, 9, :], misc_w[:, 120:128]
            act.wait_ge(for_act, 1)
            done(act.activation(soft, sm[:, 8, :], ACT.Exp, scale=-1.0))
            act.wait_ge(from_act, n_from[0])
            done(act.activation(soft, soft, ACT.Ln, bias=1.0))
            done(act.activation(expA, expA, ACT.Exp))
            act.wait_ge(for_act, 2)
            done(act.activation(sm[:, 6, :], sm[:, 4, :], ACT.Exp))
            done(act.activation(sm[:, 14, 8:16], sm[:, 14, 8:16], ACT.Exp))
            done(act.activation(sm[:, 2, :].rearrange("p (t h) -> p t h", t=NT), sm[:, 0:2, 0:8], ACT.Sigmoid))
            act.wait_ge(silu_done, 6)

            def square(u):
                if u >= 2:
                    wait_sp(act, ("norm", u - 2))
                act.activation(dn_tile(u % 2), qkvT[:, 2 * u:2 * u + 2, :].rearrange("p f (a t) -> p (f a) t", a=2),
                               ACT.Square).then_inc(act_done, 1)

            def norm(u):
                wait_sp(act, ("norm", u))
                if u >= 2:
                    act.wait_ge(for_act, 2 + u - 1)
                act.activation(dn_tile(2 + u % 2), sp_bank(("norm", u))[:, :].rearrange("p (h d) -> p h d", h=4),
                               ACT.Sqrt, bias=eps_nm[:, :]).then_inc(sp_free[K[("norm", u)] % 4], 1)
            for u in range(8):
                square(u)
                if u:
                    norm(u - 1)
            norm(7)

            def put(name, dst, n=512):
                wait_sp(act, name)
                act.activation(dst, sp_bank(name)[:, 0:n].rearrange("p (h d) -> p h d", h=4), ACT.Copy)\
                   .then_inc(sp_free[K[name] % 4], 1)

            for hh in range(2):
                put(("ktok", hh), k_tok[:, 4 * hh:4 * hh + 4, :])
            for t in range(NT):
                for hh in range(2):
                    put(("vtok", t, hh), v_tok[:, t, 4 * hh:4 * hh + 4, :])
            n_ss = 10
            for t in range(NT):
                for hh in range(2):
                    wait_sp_read(act, ("row", t, hh))
                    dt_ = dn_tile(6 * hh)
                    done(act.activation(dt_, dt_, ACT.Exp))
                for n in range(1, len(BLOCKS)):
                    for hh in range(2):
                        put(("g", t, n, hh), dn_tile(6 * hh + 5))
                for hh in range(2):
                    put(("v", t, hh), dn_tile(6 * hh + 5))
                for hh in range(2):
                    n_ss += 1
                    act.wait_ge(for_act, n_ss)
                    done(act.activation(sm[:, 11, 4 * hh:4 * hh + 4], sm[:, 10, 4 * hh:4 * hh + 4], ACT.Sqrt,
                                        bias=eps_nm[:, :], scale=1.0 / DH))
                for hh in range(2):
                    put(("y", t, hh), yt[:, 8 + 4 * hh:12 + 4 * hh, t * P:(t + 1) * P])
            for hh in range(2):
                wait_sp_read(act, ("y", 1, hh))
            outer("out0", KT)
            ln(0)
            split_xt(1)
            ffn(0)
            ln(1, stop == "l0")
            if stop == "l0":
                return

            split_xt(2)
            halves(2)
            c = C["gates"]
            b = chunk_in(c)
            for t in range(NT):
                ins = act.activation(gates[:, t, :], b[t][:, 0:48], ACT.Sigmoid)
            ins.then_inc(pair_free[c % 2], 1)
            for n in range(2):
                halves(8)
                c = C["kcvc"] + n
                b = chunk_in(c)
                for a in range(2):
                    ins = act.activation(kcT[:, n, 2 * a:2 * a + 2, :], b[a][:, :].rearrange("p (f t) -> p f t", f=2), ACT.Copy)
                ins.then_inc(pair_free[c % 2], 1)
            act.wait_ge(for_act, 15)
            for r, n in ((slice(0, P), slice(0, 2)), (slice(0, NCG), slice(2, 3))):
                m = 2 if n.start == 0 else 1
                half_n = DH // 2
                sv = sinb[r] if m == 2 else sinc[r].rearrange("p (t n) -> p t n", t=1)
                cv = cosb[r] if m == 2 else cosc[r].rearrange("p (t n) -> p t n", t=1)
                act.activation(sv[:, :, half_n:], angle[r, n, :], ACT.Sin)
                done(act.activation(cv[:, :, half_n:], turns[r, n, :], ACT.Sin, bias=half_pi[r], scale=-1.0))
            for b in range(2):
                halves(8)
                c = C["w1"] + b
                sums = chunk_in(c)[0][:, 0:128].rearrange("p (k n) -> p k n", k=2)[:, :, 0:NCG]
                if b:
                    wait_sp_read(act, ("kcmp",))
                act.activation(cmp_hT[:, :, 0:NCG], sums, ACT.Gelu_apprx_tanh).then_inc(pair_free[c % 2], 1)
            put_v = ("vcmp",)
            wait_sp(act, put_v)
            act.activation(vcmp[0:NCMP], sp_bank(put_v)[0:NCMP, :].rearrange("p (g d) -> p g d", g=NG), ACT.Copy)\
               .then_inc(sp_free[K[put_v] % 4], 1)
            n_rope = 15

            def rope_stage(c, n):
                b = chunk_in(c)
                act.wait_ge(for_act, n_rope + n)
                for t in range(NT):
                    ins = act.activation(rope_in[:, t, :], b[t][:, :], ACT.Copy)
                ins.then_inc(pair_free[c % 2], 1)
            for n in range(4):
                halves(8)
                c = C["kv"] + n
                if n % 2 == 0:
                    rope_stage(c, n // 2)
                    continue
                b = chunk_in(c)
                for t in range(NT):
                    ins = act.activation(vs[:, n // 2, t, :], b[t][:, :], ACT.Copy)
                ins.then_inc(pair_free[c % 2], 1)

            for j in range(4):
                halves(8)
                rope_stage(C["q"] + j, 2 + j)
            att = n_rope + 6
            for g in range(NG):
                for t in range(NT):
                    kn = (t + 1) * P
                    att += 1
                    act.wait_ge(for_act, att)
                    for h in range(HPG):
                        ins = act.activation(sc_cmp[:, h, :], sc_cmp[:, h, :], ACT.Exp, bias=sm[:, 4, h:h + 1],
                                             accum_out=sm[:, 5, h:h + 1])
                    done(ins)
                    for b in range(2):
                        att += 1
                        act.wait_ge(for_act, att)
                        v = sc_buf[b][:, 0:HPG * kn].rearrange("p (h n) -> p h n", h=HPG)
                        for h in range(HPG):
                            ins = act.activation(v[:, h, :], v[:, h, :], ACT.Exp, bias=sm[:, 4, 4 + 4 * b + h:5 + 4 * b + h],
                                                 accum_out=sm[:, 5, 4 + 4 * b + h:5 + 4 * b + h])
                        done(ins)
                    name = ("cT", g, t)
                    wait_sp(act, name)
                    act.activation(pT_cmp[0:NCMP], sp_bank(name)[0:NCMP, :], ACT.Copy).then_inc(sp_free[K[name] % 4], 1)
                    for b in range(2):
                        for k in range(t + 1):
                            name = ("pT", g, t, b, k)
                            wait_sp(act, name)
                            act.activation(pT_buf[b][:, k, :], sp_bank(name)[:, :], ACT.Copy).then_inc(sp_free[K[name] % 4], 1)
                    put(("oT", g, t), yt[:, 4 * g:4 * g + 4, t * P:(t + 1) * P])
            for t in range(NT):
                wait_sp_read(act, ("oT", NG - 1, t))
            outer("out1", KT)
            ln(2)
            split_xt(3)
            ffn(1)
            ln(3, True)

        @block.vector
        def _(dv):
            h_next = [0]
            n_own, n_pe, n_act = [0], [0], [0]

            def own(ins, i=None, per=0):
                n_own[0] += 1
                ins.then_inc(dve, 1)
                dv.wait_ge(dve, at(n_own[0], i, per))

            def to_act(ins):
                n_act[0] += 1
                ins.then_inc(for_act, 1)

            marks = [0]

            def mark():
                marks[0] += 1
                return dv.memset(sm[:, 0, marks[0] % 16:marks[0] % 16 + 1], 0.0)

            def to_pe(ins, name):
                n_pe[0] += 1
                assert FP[name] == n_pe[0]
                ins.then_inc(for_pe, 1)

            def halves(count, i=None, per=0):
                for _ in range(count):
                    h = h_next[0]
                    if h >= 2 * total_slabs:
                        return
                    src, slot, n = half_of(h)
                    dv.wait_ge(w_hi_ready, at(h + 1, i, per))
                    dv.tensor_tensor(w_lo[:, slot, 0:n], src, w_hi[:, slot, 0:n].bitcast(F32), ALU.subtract)\
                      .then_inc(w_lo_ready, 1)
                    h_next[0] += 1

            def loop_over(n, per_halves, body, per_own=0):
                o = n_own[0]
                with dv.Fori(0, n) as i:
                    body(i)
                assert n_own[0] == o + per_own
                n_own[0] += (n - 1) * per_own
                h_next[0] += (n - 1) * per_halves

            def chunk_in(c, i=None, per=0):
                dv.wait_ge(half_used, at(chunk_end[c], i, 16 * per))
                return pair(c)

            def chunk_staged(c, i=None, per=0):
                dv.wait_ge(pair_free[c % 2], at(c // 2 + 1, i, per))

            def bc(ap, n):
                return ap.unsqueeze(1).to_broadcast([ap.shape[0], n, ap.shape[-1]])

            def over(ap, n):
                return ap.unsqueeze(2).to_broadcast([ap.shape[0], ap.shape[1], n])

            def split_xt(m):
                if m:
                    dv.wait_ge(gb_in, 48 * m)
                for q in range(4):
                    for u in (2 * q, 2 * q + 1):
                        name = ("xT", m, u)
                        wait_sp(dv, name)
                        for a in range(2):
                            kt = 2 * u + a
                            src = sp_bank(name)[:, a * SEQ:(a + 1) * SEQ]
                            if m == 0:
                                ins = dv.tensor_copy(yt[:, kt, :], src)
                            else:
                                ins = dv.tensor_scalar(yt[:, kt, :], src, lnT[:, 0, kt:kt + 1], lnT[:, 1, kt:kt + 1],
                                                       ALU.mult, ALU.add)
                        ins.then_inc(sp_free[K[name] % 4], 1)
                    dv.wait_ge(xt_hi_ready, 4 * m + q + 1)
                    v = slice(4 * q, 4 * q + 4)
                    dv.tensor_tensor(xt_lo[:, v, :], yt[:, v, :], xt_hi[:, v, :].bitcast(F32), ALU.subtract)\
                      .then_inc(xt_lo_ready, 1)

            def outer(name, n):
                src = outer_src(name)

                def split(kt, i=None):
                    dv.wait_ge(a_hi_ready, at(A0[name] + kt + 1, i, 4))
                    col = kt if i is None else ds(i * 4 + kt, 1)
                    s_ = src[:, col, :]
                    dv.tensor_tensor(a_lo[:, kt % 4, :], s_, a_hi[:, kt % 4, :].bitcast(F32), ALU.subtract)\
                      .then_inc(a_lo_ready, 1)

                def quad(kt, i=None):
                    for j in range(4):
                        if kt + j + 1 < n:
                            split(kt + j + 1, i)
                        halves(2, i, 8)
                split(0)
                loop_over(n // 4 - 1, 8, lambda i: quad(0, i))
                quad(n - 4)

            def ln(n, last=False):
                name = ("out0", "fout0", "out1", "fout1")[n]
                if n:
                    dv.wait_ge(x_scaled, NT * n)
                else:
                    dv.wait_ge(x_in_sem, 16 * NT)

                def add(t):
                    for c in range(4):
                        v = x[:, t, c * CH:(c + 1) * CH]
                        ins = dv.scalar_tensor_tensor(v, v, ALPHA, bank[4 * t + c][:, :], ALU.mult, ALU.add)
                    own(ins)

                def moments(t):
                    for c in range(4):
                        ins = dv.bn_stats(stats[:, t, c, :], x[:, t, c * CH:(c + 1) * CH])
                    own(ins)
                    dv.bn_aggr(mv[:, t, :], stats[:, t, :, :].rearrange("p c s -> p (c s)")).then_inc(var_ready, 1)

                def scale(t):
                    dv.wait_ge(std_ready, NT * n + t + 1)
                    own(dv.reciprocal(rstd[:, t:t + 1], rstd[:, t:t + 1]))
                    if not last:
                        dv.scalar_tensor_tensor(nmr[:, t:t + 1], mv[:, t, 0:1], -1.0, rstd[:, t:t + 1], ALU.mult, ALU.mult)\
                          .then_inc(nmr_ready, 1)

                def result(t):
                    for c in range(2):
                        v, w = x[:, t, c * D // 2:(c + 1) * D // 2], slice(c * D // 2, (c + 1) * D // 2)
                        own(dv.scalar_tensor_tensor(v, v, mv[:, t, 0:1], gb[:, 0, w], ALU.subtract, ALU.mult))
                        dv.scalar_tensor_tensor(v, v, rstd[:, t:t + 1], gb[:, 1, w], ALU.mult, ALU.add).then_inc(out_ready, 1)

                dv.wait_ge(first_whole, n + 1)
                add(0)
                moments(0)
                dv.wait_ge(half_used, 2 * (S[name] + (FT if n % 2 else KT)))
                add(1)
                scale(0)
                moments(1)
                if last:
                    dv.wait_ge(gb_in, 48 * (n + 1))
                    result(0)
                scale(1)
                if last:
                    result(1)

            def ffn(layer):
                c0, k0 = C[f"ffn{layer}"], K[("ffn", layer, 0)]
                n_hid = layer * (FFN // CH)

                def up(c, k, first, i=None):
                    chunk_staged(c - 1, i, 2)
                    b = chunk_in(c, i, 2)
                    if not first:
                        for a in range(2):
                            dv.wait_ge(sp_ready[(k - 2 + a) % 4], at((k - 2 + a) // 4 + 1, i, 1))
                    for t in range(NT):
                        ins = dv.tensor_tensor(hid[:, t, :], b[t][:, :], sg[:, t, :], ALU.mult)
                        ins.then_inc(hid_ready if t else pair_free[c % 2], 1)
                halves(16)
                up(c0 + 1, k0, True)

                def body(i):
                    for n in range(2):
                        halves(16, i, 32)
                        up(c0 + 3 + 2 * n, k0 + 2 + 2 * n, False, i)
                loop_over(5, 32, body)
                outer(f"fout{layer}", FT)

            dv.memset(sm[:, 15, :], 0.0).then_inc(stage_free, 2)
            halves(LEAD)
            split_xt(0)
            dv.wait_ge(consts, 3)
            halves(2)
            halves(8 * 2)
            dv.wait_ge(small_in, 16 * 5)

            def conv(dst, src, w, taps, i=None, per=0):
                for tap in range(taps):
                    for f in range(4):
                        wv = w(f, taps - 1 - tap)
                        if tap == 0:
                            ins = dv.tensor_scalar(dst[:, f, :], src[:, f, :], wv, None, ALU.mult)
                        else:
                            ins = dv.scalar_tensor_tensor(dst[:, f, tap:], src[:, f, 0:SEQ - tap], wv, dst[:, f, tap:],
                                                          ALU.mult, ALU.add)
                    if tap < taps - 1:
                        own(ins, i, per)
                ins.then_inc(stage_free, 1)

            def qkv_turn(i):
                for j in range(2):
                    halves(8, i, 16)
                    chunk_staged(C["qkv"] + j, i, 1)

                    def w(f, tap):
                        return misc_w[:, ds(i * 32 + 16 * j + 4 * f + tap, 1)]
                    conv(qkvT[:, ds(i * 8 + 4 * j, 4), :], conv_in[:, j, :, :], w, DNK, i, 6)
            loop_over(3, 16, qkv_turn, per_own=6)
            for j in range(2):
                halves(8)
                halves(8)
                c = C["sc"] + 3 * j
                chunk_staged(c)
                b = chunk_in(c + 1)
                for a in range(2):
                    v = conv_in[:, j, 2 * a:2 * a + 2, :].rearrange("p f t -> p (f t)")
                    ins = dv.tensor_tensor(v, v, b[a][:, :], ALU.mult)
                ins.then_inc(pair_free[(c + 1) % 2], 1)
                dv.wait_ge(pair_free[(c + 1) % 2], (c + 1) // 2 + 1)
                conv(conv_out, conv_in[:, j, :, :], lambda f, tap: misc_w[:, 96 + 3 * (4 * j + f) + tap:97 + 3 * (4 * j + f) + tap], SCK)
                halves(8)
                dv.wait_ge(stage_free, 9 + j)
                b = chunk_in(c + 2)
                for a in range(2):
                    v = conv_out[:, 2 * a:2 * a + 2, :].rearrange("p f t -> p (f t)")
                    ins = dv.tensor_tensor(yt[:, 4 * j + 2 * a:4 * j + 2 * a + 2, :].rearrange("p f t -> p (f t)"), v, b[a][:, :], ALU.mult)
                ins.then_inc(pair_free[(c + 2) % 2], 1)

            s_, abs_, g_ = sm[:, 15, :], sm[:, 8, :], sm[:, 3, :]

            def th(ap):
                return ap.rearrange("p (t h) -> p t h", t=NT)
            own(dv.tensor_tensor(th(s_), sm[:, 0:2, 8:16], bc(misc_w[:, 128:136], NT), ALU.add))
            to_act(dv.scalar_tensor_tensor(abs_, s_, -1.0, s_, ALU.mult, ALU.max))
            dv.wait_ge(from_act, 3)
            own(dv.scalar_tensor_tensor(s_, s_, 0.0, sm[:, 9, :], ALU.max, ALU.add))
            to_pe(dv.scalar_tensor_tensor(th(g_), th(s_), -1.0, bc(misc_w[:, 120:128], NT), ALU.mult, ALU.mult), ("g",))
            name = ("gc",)
            wait_sp(dv, name)
            b = sp_bank(name)
            gc_, ngc, egc, nbe, beta, kdec = sm[:, 4, :], sm[:, 5, :], sm[:, 6, :], sm[:, 7, :], sm[:, 2, :], sm[:, 14, 8:16]
            own(dv.tensor_copy(gc_, b[:, 0:16]))
            own(dv.tensor_scalar(ngc, gc_, -1.0, None, ALU.mult))
            dv.tensor_tensor(kdec, b[:, 16:24], gc_[:, 0:8], ALU.subtract).then_inc(sp_free[K[name] % 4], 1)
            dv.wait_ge(sp_free[K[name] % 4], K[name] // 4 + 1)
            to_act(dv.tensor_copy(sm[:, 15, 0:8], kdec))
            dv.wait_ge(from_act, 6)
            own(dv.scalar_tensor_tensor(nbe, egc, -1.0, beta, ALU.mult, ALU.mult))
            zf = z_tok.rearrange("p t h d -> p (t h) d")
            own(dv.tensor_tensor(zf, zf, bc(norm_w, NT * DNH), ALU.mult))
            for u in range(8):
                name = ("norm", u)
                wait_sp_read(dv, name)
                r = dn_tile(2 + u % 2).rearrange("p h d -> p (h d)")
                v = qkvT[:, 2 * u:2 * u + 2, :].rearrange("p f t -> p (f t)")
                own(dv.reciprocal(r, r))
                to_act(dv.scalar_tensor_tensor(v, r, SCALE if u < 4 else 1.0, v, ALU.mult, ALU.mult))
            to_pe(mark(), ("kn",))
            for hh in range(2):
                wait_sp_read(dv, ("ktok", hh))
            own(dv.tensor_tensor(k_tok, k_tok, over(kdec, DH), ALU.mult))
            for t in range(NT):
                for hh in range(2):
                    wait_sp_read(dv, ("vtok", t, hh))
            n_from = [6]

            def sp_out(ins, name):
                ins.then_inc(sp_free[K[name] % 4], 1)

            def sp4(name):
                return sp_bank(name)[:, :].rearrange("p (h d) -> p h d", h=4)
            for t in range(NT):
                heads = [slice(8 * t + 4 * hh, 8 * t + 4 * hh + 4) for hh in range(2)]
                tiles = [[dn_tile(6 * hh + n) for n in range(6)] for hh in range(2)]
                for hh in range(2):
                    _, _, _, T, _, G = tiles[hh]
                    if t:
                        wait_sp(dv, ("y", 0, hh))
                    dv.tensor_tensor(G, bc(upper[:, :], 4), over(g_[:, heads[hh]], P), ALU.mult)
                    to_pe(dv.tensor_tensor(T, bc(ident[:, :], 4), over(beta[:, heads[hh]], P), ALU.mult), ("rows", t, hh))
                for hh in range(2):
                    Dt, AT, E, T, X, G = tiles[hh]
                    name = ("row", t, hh)
                    wait_sp(dv, name)
                    for h in range(4):
                        n = 8 * t + 4 * hh + h
                        ins = dv.scalar_tensor_tensor(Dt[:, h, :], sp4(name)[:, h, :], ngc[:, n:n + 1], neg_lower[:, :], ALU.add, ALU.add)
                    sp_out(ins, name)
                    n_from[0] += 1
                    dv.wait_ge(from_act, n_from[0])
                    wait_sp(dv, ("kk", t, hh))
                    sp_out(dv.tensor_tensor(AT, sp4(("kk", t, hh)), Dt, ALU.mult), ("kk", t, hh))
                    wait_sp_read(dv, ("kk", t, hh))
                    wait_sp(dv, ("beta", t, hh))
                    sp_out(dv.tensor_tensor(AT, AT, sp4(("beta", t, hh)), ALU.mult), ("beta", t, hh))
                    wait_sp(dv, ("kq", t, hh))
                    sp_out(dv.tensor_tensor(Dt, Dt, sp4(("kq", t, hh)), ALU.mult), ("kq", t, hh))
                    wait_sp_read(dv, ("beta", t, hh))
                    own(dv.tensor_tensor(E, AT, bc(blk_mask[:, 0, :], 4), ALU.mult))
                    to_pe(dv.tensor_tensor(X, bc(ident[:, :], 4), E, ALU.subtract), ("m", t, 0, hh))
                for hh in range(2):
                    Dt, AT, E, T, X, G = tiles[hh]
                    name = ("eT", t, hh)
                    wait_sp(dv, name)
                    sp_out(dv.tensor_tensor(T, bc(ident[:, :], 4), sp4(name), ALU.subtract), name)
                    to_pe(dv.tensor_tensor(E, AT, bc(blk_mask[:, 1, :], 4), ALU.mult), ("m", t, 1, hh))
                for n in range(1, len(BLOCKS)):
                    for hh in range(2):
                        Dt, AT, E, T, X, G = tiles[hh]
                        wait_sp(dv, ("x", t, n, hh))
                        if n < len(BLOCKS) - 1:
                            wait_sp(dv, ("t", t, n, hh))
                            sp_out(dv.tensor_tensor(X, X, sp4(("x", t, n, hh)), ALU.subtract), ("x", t, n, hh))
                            sp_out(dv.tensor_tensor(T, T, sp4(("t", t, n, hh)), ALU.subtract), ("t", t, n, hh))
                            to_pe(dv.tensor_tensor(E, AT, bc(blk_mask[:, n + 1, :], 4), ALU.mult), ("m", t, n + 1, hh))
                        else:
                            sp_out(dv.tensor_tensor(X, X, sp4(("x", t, n, hh)), ALU.subtract), ("x", t, n, hh))
                for hh in range(2):
                    Dt, AT, E, T, X, G = tiles[hh]
                    ins = dv.tensor_tensor(T, v_tok[:, t, 4 * hh:4 * hh + 4, :], over(beta[:, heads[hh]], DH), ALU.mult)
                    if t == 0:
                        to_pe(ins, ("rhs", t, hh))
                        continue
                    own(ins)
                    wait_sp(dv, ("ks", hh))
                    for h in range(4):
                        n = 8 * t + 4 * hh + h
                        ins = dv.scalar_tensor_tensor(T[:, h, :], sp4(("ks", hh))[:, h, :], nbe[:, n:n + 1], T[:, h, :], ALU.mult, ALU.add)
                    sp_out(ins, ("ks", hh))
                    wait_sp(dv, ("qs", hh))
                    sp_out(dv.tensor_tensor(AT, sp4(("qs", hh)), over(egc[:, heads[hh]], DH), ALU.mult), ("qs", hh))
                    wait_sp_read(dv, ("ks", hh))
                    wait_sp_read(dv, ("qs", hh))
                    to_pe(mark(), ("rhs", t, hh))
                for hh in range(2):
                    Dt, AT, E, T, X, G = tiles[hh]
                    name = ("o", t, hh)
                    wait_sp(dv, name)
                    if t:
                        sp_out(dv.tensor_tensor(AT, AT, sp4(name), ALU.add), name)
                    else:
                        sp_out(dv.tensor_copy(AT, sp4(name)), name)
                        wait_sp(dv, ("s", hh))
                        sp_out(dv.tensor_copy(state[:, 4 * hh:4 * hh + 4, :], sp4(("s", hh))), ("s", hh))
                    wait_sp_read(dv, name)
                    own(dv.tensor_tensor(E, AT, AT, ALU.mult))
                    to_act(dv.tensor_reduce(sm[:, 10, 4 * hh:4 * hh + 4], E, AX.X, ALU.add))
                for hh in range(2):
                    Dt, AT, E, T, X, G = tiles[hh]
                    n_from[0] += 1
                    dv.wait_ge(from_act, n_from[0])
                    r = sm[:, 11, 4 * hh:4 * hh + 4]
                    own(dv.reciprocal(r, r))
                    for h in range(4):
                        ins = dv.scalar_tensor_tensor(AT[:, h, :], AT[:, h, :], r[:, h:h + 1], z_tok[:, t, 4 * hh + h, :], ALU.mult, ALU.mult)
                    to_pe(ins, ("on", t, hh))
            for hh in range(2):
                wait_sp(dv, ("y", 1, hh))
            mark().then_inc(gb_free, 1)
            outer("out0", KT)
            ln(0)
            split_xt(1)
            mark().then_inc(gb_free, 1)
            ffn(0)
            ln(1, stop == "l0")
            if stop == "l0":
                return

            split_xt(2)
            halves(2)
            dv.wait_ge(nsa_in, 16 * 10)
            rows = [(slice(0, P), slice(0, 2)), (slice(0, NCG), slice(2, 3))]
            for r, n in rows:
                for a in range(n.start, n.stop):
                    own(dv.tensor_copy(sm[r, 15, a:a + 1], angle[r, a, 0:1].bitcast(I32)))
                    own(dv.tensor_scalar(angle[r, a, :], turns[r, a, :], sm[r, 15, a:a + 1], None, ALU.mult))
                av, tv = angle[r, n, :], turns[r, n, :]
                own(dv.tensor_scalar(tv, av, float(1 / (2 * np.pi)), ROUND, ALU.mult, ALU.add))
                own(dv.tensor_scalar(tv, tv, ROUND, None, ALU.subtract))
                for part_ in (TWO_PI_1, TWO_PI_2, TWO_PI_3):
                    own(dv.scalar_tensor_tensor(av, tv, -part_, av, ALU.mult, ALU.add))
                own(dv.tensor_scalar(av, av, PI, -PI, ALU.min, ALU.max))
                ins = dv.scalar_tensor_tensor(tv, av, -1.0, av, ALU.mult, ALU.max)
                if n.start == 0:
                    own(ins)
            to_act(ins)
            halves(8)
            halves(8)
            dv.wait_ge(from_act, 16)
            n_from[0] = 16
            hd = DH // 2
            for cv, sv in ((cosb, sinb), (cosc[0:NCG].unsqueeze(1), sinc[0:NCG].unsqueeze(1))):
                own(dv.tensor_copy(cv[:, :, 0:hd], cv[:, :, hd:]))
                own(dv.tensor_scalar(sv[:, :, 0:hd], sv[:, :, hd:], -1.0, None, ALU.mult))
            dv.wait_ge(x_scaled, 2 * NT)
            for b in range(2):
                chunk_staged(C["kcvc"] + b)
                if b:
                    dv.wait_ge(half_used, 2 * S["w1"] + 8)
                for hf in range(2):
                    lo = slice(16 * hf, 16 * hf + 16)
                    for g in range(NG):
                        src = kcT[:, b, g, 16 * hf:16 * hf + 16 * NCMP].rearrange("p (n l) -> p l n", l=16)
                        ins = dv.tensor_tensor(blk_sum[:, lo, g * NCMP:(g + 1) * NCMP], src, over(posT[:, b, lo], NCMP), ALU.add)
                own(ins)
                own(dv.tensor_copy(blk_hi[:, :, :], blk_sum))
                to_pe_ins = dv.tensor_tensor(blk_lo[:, :, :], blk_sum, blk_hi[:, :, :].bitcast(F32), ALU.subtract)
                to_pe_ins.then_inc(for_pe, 1)
                halves(8)
            name = ("kcmp",)
            wait_sp(dv, name)
            kb = sp_bank(name)
            rows_ = slice(0, NCG)
            ra, rb = rope_a[rows_, 0, 0:DH], rope_b[rows_, 0, 0:DH]
            dv.tensor_tensor(ra, kb[rows_, 0:DH], cosc[rows_], ALU.mult)
            dv.tensor_tensor(rb[:, 0:hd], kb[rows_, hd:DH], sinc[rows_, 0:hd], ALU.mult)
            sp_out(dv.tensor_tensor(rb[:, hd:DH], kb[rows_, 0:hd], sinc[rows_, hd:DH], ALU.mult), name)
            wait_sp_read(dv, name)
            dv.tensor_tensor(ra, ra, rb, ALU.add).then_inc(for_pe, 1)
            name = ("kcmpT",)
            wait_sp(dv, name)
            sp_out(dv.tensor_copy(kcmpT[:, 0:NCG], sp_bank(name)[:, 0:NCG]), name)

            def rope(c):
                chunk_staged(c)
                for t in range(NT):
                    v = rope_in[:, t, :].rearrange("p (h d) -> p h d", h=4)
                    va = rope_a[:, t, :].rearrange("p (h d) -> p h d", h=4)
                    vb = rope_b[:, t, :].rearrange("p (h d) -> p h d", h=4)
                    dv.tensor_tensor(va, v, bc(cosb[:, t, :], 4), ALU.mult)
                    dv.tensor_tensor(vb[:, :, 0:hd], v[:, :, hd:DH], bc(sinb[:, t, 0:hd], 4), ALU.mult)
                    ins = dv.tensor_tensor(vb[:, :, hd:DH], v[:, :, 0:hd], bc(sinb[:, t, hd:DH], 4), ALU.mult)
                to_act(ins)
                dv.wait_ge(for_act, n_act[0])
                dv.tensor_tensor(rope_a, rope_a, rope_b, ALU.add).then_inc(for_pe, 1)

            def put_T(k, dst):
                for a in range(2):
                    dv.wait_ge(sp_ready[(k + a) % 4], (k + a) // 4 + 1)
                    dv.tensor_copy(dst(a), bank[4 + (k + a) % 4][:, :].rearrange("p (h t) -> p h t", h=2)).then_inc(sp_free[(k + a) % 4], 1)
            for b in range(2):
                halves(8)
                rope(C["kv"] + 2 * b)
                halves(8)
                put_T(K[("kv", b, 0)], lambda a: ksT[:, b, 2 * a:2 * a + 2, :])

            for j in range(4):
                halves(8)
                rope(C["q"] + j)
                put_T(K[("q", 2 * j)], lambda a: qT[:, 4 * j + 2 * a:4 * j + 2 * a + 2, :])
            assert n_act[0] == 21
            nmax, sums, cf = sm[:, 4, :], sm[:, 5, :], sm[:, 6, :]
            gate_v = gates.rearrange("p t (h b) -> p t h b", b=3)
            for g in range(NG):
                for t in range(NT):
                    kn = (t + 1) * P
                    if g or t:
                        wait_sp(dv, ("co", *((g, 0) if t else (g - 1, 1))))
                    name = ("c", g, t)
                    wait_sp(dv, name)
                    v = sp_bank(name)[:, 0:HPG * NCMP].rearrange("p (h n) -> p h n", h=HPG)
                    sp_out(dv.scalar_tensor_tensor(sc_cmp, v, SCALE, bc(neg_cmp[:, t, :], HPG), ALU.mult, ALU.add), name)
                    wait_sp_read(dv, name)
                    to_act(dv.tensor_reduce(nmax[:, 0:4], sc_cmp, AX.X, ALU.max, negate=True))
                    for b in range(2):
                        v = sc_buf[b][:, 0:HPG * kn].rearrange("p (h n) -> p h n", h=HPG)
                        hp = HPG // (t + 1)
                        for k in range(t + 1):
                            name = ("s", g, t, b, k)
                            wait_sp(dv, name)
                            mask = neg_upper.rearrange("p a n -> p (a n)")[:, SEQ - kn:SEQ]
                            sp_out(dv.scalar_tensor_tensor(v[:, hp * k:hp * k + hp, :], sp_bank(name)[:, :].rearrange("p (h n) -> p h n", h=hp),
                                                           SCALE, bc(mask, hp), ALU.mult, ALU.add), name)
                        for k in range(t + 1):
                            wait_sp_read(dv, ("s", g, t, b, k))
                        to_act(dv.tensor_reduce(nmax[:, 4 + 4 * b:8 + 4 * b], v, AX.X, ALU.max, negate=True))
                    n_from[0] += 1
                    dv.wait_ge(from_act, n_from[0])
                    dv.tensor_tensor(sc_cmp, sc_cmp, bc(ok_cmp[:, t, :], HPG), ALU.mult).then_inc(for_pe, 1)
                    n_from[0] += 2
                    dv.wait_ge(from_act, n_from[0])
                    own(dv.reciprocal(cf[:, 0:12], sums[:, 0:12]))
                    own(dv.tensor_tensor(cf[:, 0:12].rearrange("p (b h) -> p b h", b=3), cf[:, 0:12].rearrange("p (b h) -> p b h", b=3),
                                         gate_v[:, t, 4 * g:4 * g + 4, :].rearrange("p h b -> p b h"), ALU.mult))
                    if g or t:
                        wait_sp(dv, ("oT", *((g, 0) if t else (g - 1, 1))))
                    for b, name in enumerate((("co", g, t), ("po", g, t, 0), ("po", g, t, 1))):
                        wait_sp(dv, name)
                        for h in range(HPG):
                            w = cf[:, 4 * b + h:4 * b + h + 1]
                            if b == 0:
                                ins = dv.tensor_scalar(o_buf[:, h, :], sp4(name)[:, h, :], w, None, ALU.mult)
                            else:
                                ins = dv.scalar_tensor_tensor(o_buf[:, h, :], sp4(name)[:, h, :], w, o_buf[:, h, :], ALU.mult, ALU.add)
                        sp_out(ins, name)
                        wait_sp_read(dv, name)
                    mark().then_inc(for_pe, 1)
            mark().then_inc(gb_free, 1)
            outer("out1", KT)
            ln(2)
            split_xt(3)
            mark().then_inc(gb_free, 1)
            ffn(1)
            ln(3, True)

        @block.tensor
        def _(pe):
            n_pe = [0]

            def sp_use(name, i=None, per=0):
                k = K[name]
                if k >= 4:
                    pe.wait_ge(sp_free[k % 4], at(k // 4, i, per // 4))
                return bank[4 + k % 4]

            def sp_done(ins, name):
                ins.then_inc(sp_ready[K[name] % 4], 1)

            def handed(name):
                pe.wait_ge(for_pe, FP[name])

            def used(ins, h=None):
                ins.then_inc(half_used, 1)

            def passes(dst, l_hi, l_lo, r_hi, r_lo, start, stop, shared=False):
                pe.matmul(dst, l_hi, r_hi, start=start, stop=False, skip_group_check=shared)
                pe.matmul(dst, l_hi, r_lo, start=False, stop=False, skip_group_check=shared)
                return pe.matmul(dst, l_lo, r_hi, start=False, stop=stop, skip_group_check=shared)

            def xT(m):
                if m == 0:
                    pe.wait_ge(ident_ready, 1)
                    pe.wait_ge(x_in_sem, 16 * NT)
                for u in range(8):
                    if m and u % 2 == 0:
                        pe.wait_ge(x_normed, 5 * (m - 1) + 2 + u // 2)
                    name = ("xT", m, u)
                    b = sp_use(name)
                    for a in range(2):
                        for t in range(NT):
                            ins = pe.transpose(b[:, a * SEQ + t * P:a * SEQ + (t + 1) * P],
                                               x[:, t, (2 * u + a) * P:(2 * u + a + 1) * P], ident[:, :])
                    sp_done(ins, name)

            def slab_in_chunk(s, quad, b, by_token, i, per, m=None):
                if m is not None:
                    pe.wait_ge(xt_lo_ready, 4 * m + quad + 1)
                for hf in range(2):
                    h = 2 * (s + quad) + hf
                    pe.wait_ge(w_lo_ready, at(h + 1, i, 2 * per))
                    for kk in range(2):
                        kt = 4 * quad + 2 * hf + kk
                        cols = slice(kk * CH, (kk + 1) * CH)
                        hi, lo = w_hi[:, h % HL_SLOTS, cols], w_lo[:, h % HL_SLOTS, cols]
                        if by_token:
                            for t in range(NT):
                                v = slice(t * P, (t + 1) * P)
                                ins = passes(b[t][:, :], xt_hi[:, kt, v], xt_lo[:, kt, v], hi, lo, kt == 0, kt == KT - 1)
                        else:
                            for f in range(4):
                                v = slice(f * P, (f + 1) * P)
                                ins = passes(b[f // 2][:, f % 2 * SEQ:(f % 2 + 1) * SEQ], hi[:, v], lo[:, v],
                                             xt_hi[:, kt, :], xt_lo[:, kt, :], kt == 0 and f % 2 == 0, kt == KT - 1, True)
                    if quad == 3 and hf == 1:
                        return ins
                    used(ins)

            def chunk(s, c, by_token, i=None, per=0, between=None, m=None):
                if c >= 2:
                    pe.wait_ge(pair_free[c % 2], at(c // 2, i, per // 2))
                b = pair(c)
                for quad in range(4):
                    ins = slab_in_chunk(s, quad, b, by_token, i, 4 * per, m)
                    if quad == 0 and between:
                        between()
                used(ins)

            def small(s, c, n, m):
                if c >= 2:
                    pe.wait_ge(pair_free[c % 2], c // 2)
                b = pair(c)
                for hf in range(2):
                    h = 2 * s + hf
                    pe.wait_ge(w_lo_ready, h + 1)
                    for kk in range(KT // 2):
                        kt = hf * (KT // 2) + kk
                        if kt % 4 == 0:
                            pe.wait_ge(xt_lo_ready, 4 * m + kt // 4 + 1)
                        cols = slice(kk * n, (kk + 1) * n)
                        for t in range(NT):
                            v = slice(t * P, (t + 1) * P)
                            ins = passes(b[t][:, 0:n], xt_hi[:, kt, v], xt_lo[:, kt, v], w_hi[:, h % HL_SLOTS, cols],
                                         w_lo[:, h % HL_SLOTS, cols], kt == 0, kt == KT - 1)
                    used(ins)

            def outer(name, n, layer):
                for b in range(4):
                    last = max(k for k in ks_before[name] if k % 4 == b)
                    pe.wait_ge(sp_free[b], last // 4 + 1)
                c = chunks_before[name]
                for p in range(2):
                    pe.wait_ge(pair_free[p], (c - p + 1) // 2)

                def tile(kt, tokens, i=None):
                    pe.wait_ge(a_lo_ready, at(A0[name] + kt + 1, i, 4))
                    for hf in range(2):
                        h = 2 * (S[name] + kt) + hf
                        pe.wait_ge(w_lo_ready, at(h + 1, i, 8))
                        for cc in range(2):
                            cols = slice(cc * CH, (cc + 1) * CH)
                            for t in tokens:
                                v = slice(t * P, (t + 1) * P)
                                ins = passes(bank[4 * t + 2 * hf + cc][:, :], a_hi[:, kt % 4, v], a_lo[:, kt % 4, v],
                                             w_hi[:, h % HL_SLOTS, cols], w_lo[:, h % HL_SLOTS, cols],
                                             i is None and kt == 0, i is None and kt == n - 1)
                        if tokens[-1] == NT - 1:
                            used(ins)
                    return ins

                for kt in range(4):
                    tile(kt, range(NT))
                with pe.Fori(0, n // 4 - 2) as i:
                    for kt in range(4, 8):
                        tile(kt, range(NT), i)
                for kt in range(n - 4, n - 2):
                    tile(kt, range(NT))
                for t in range(NT):
                    for kt in range(n - 2, n):
                        ins = tile(kt, range(t, t + 1))
                        if t == 0 and kt == n - 1:
                            ins.then_inc(first_whole, 1)

            def ffn(layer):
                s0, c0 = S[f"ffn{layer}"], C[f"ffn{layer}"]
                n_hid = layer * (FFN // CH)

                def hidden_T(pair_no, n_h, i=None):
                    pe.wait_ge(hid_ready, at(n_h, i, 2))
                    for a in range(2):
                        name = ("ffn", layer, 2 * pair_no + a)
                        b = sp_use(name, i, 4)
                        for f in range(2):
                            for t in range(NT):
                                ins = pe.transpose(b[:, f * SEQ + t * P:f * SEQ + (t + 1) * P],
                                                   hid[:, t, (2 * a + f) * P:(2 * a + f + 1) * P], ident[:, :])
                        sp_done(ins, name)
                for n in range(2):
                    chunk(s0 + 4 * n, c0 + n, True, m=None if n else 2 * layer + 1)
                with pe.Fori(0, 5) as i:
                    for n in range(2):
                        chunk(s0 + 8 + 8 * n, c0 + 2 + 2 * n, True, i, 4, lambda: hidden_T(n, n_hid + n + 1, i))
                        chunk(s0 + 12 + 8 * n, c0 + 3 + 2 * n, True, i, 4)
                hidden_T(10, n_hid + 11)
                outer(f"fout{layer}", FT, layer)

            order = {"out0": ("y", 1, 1), "fout0": ("ffn", 0, 21), "out1": ("oT", NG - 1, NT - 1), "fout1": ("ffn", 1, 21)}
            ks_before = {n: range(K[last] + 1) for n, last in order.items()}
            chunks_before = {"out0": C["ffn0"], "fout0": C["gates"], "out1": C["ffn1"], "fout1": C["fout1"]}

            xT(0)
            small(S["ba"], C["ba"], 16, 0)
            for j in range(2):
                chunk(S["z"] + 4 * j, C["z"] + j, True)
            with pe.Fori(0, 3) as i:
                for j in range(2):
                    chunk(S["qkv"] + 4 * j, C["qkv"] + j, False, i, 2)
            for n in range(6):
                chunk(S["sc"] + 4 * n, C["sc"] + n, False)

            handed(("g",))
            b = sp_use(("gc",))
            pe.matmul(b[:, 0:16], upper[:, :], sm[:, 3, :], start=True, stop=True)
            sp_done(pe.matmul(b[:, 16:24], ones[:, :], sm[:, 3, 0:8], start=True, stop=True), ("gc",))
            for u in range(8):
                pe.wait_ge(act_done, u + 1)
                name = ("norm", u)
                b = sp_use(name)
                sp_done(pe.matmul(b[:, :], ones[:, :], dn_tile(u % 2).rearrange("p h d -> p (h d)"), start=True, stop=True), name)
            handed(("kn",))

            def transposes(name, srcs, rows=P):
                b = sp_use(name)
                for h, src in enumerate(srcs):
                    ins = pe.transpose(b[0:rows, h * P:(h + 1) * P], src, ident[:, :])
                sp_done(ins, name)
            for hh in range(2):
                transposes(("ktok", hh), [qkvT[:, 8 + 4 * hh + h, 0:P] for h in range(4)])
            for t in range(NT):
                for hh in range(2):
                    transposes(("vtok", t, hh), [vT[:, 4 * hh + h, t * P:(t + 1) * P] for h in range(4)])

            def by_head(name, lhs, rhs):
                b = sp_use(name)
                for h in range(4):
                    ins = pe.matmul(b[:, h * P:(h + 1) * P], lhs(h), rhs(h), start=True, stop=True)
                sp_done(ins, name)

            def flat(tile):
                return tile.rearrange("p h d -> p (h d)")
            for t in range(NT):
                v = slice(t * P, (t + 1) * P)
                tiles = [[dn_tile(6 * hh + n) for n in range(6)] for hh in range(2)]
                for hh in range(2):
                    _, _, _, T, _, G = tiles[hh]
                    handed(("rows", t, hh))
                    for name, m in (("row", G), ("beta", T)):
                        b = sp_use((name, t, hh))
                        sp_done(pe.matmul(b[:, :], ones[:, :], flat(m), start=True, stop=True), (name, t, hh))
                    by_head(("kk", t, hh), lambda h: qkvT[:, 8 + 4 * hh + h, v], lambda h: qkvT[:, 8 + 4 * hh + h, v])
                    by_head(("kq", t, hh), lambda h: qkvT[:, 8 + 4 * hh + h, v], lambda h: qkvT[:, 4 * hh + h, v])
                for hh in range(2):
                    handed(("m", t, 0, hh))
                    transposes(("eT", t, hh), [tiles[hh][2][:, h, :] for h in range(4)])
                for n in range(1, len(BLOCKS)):
                    for hh in range(2):
                        _, _, E, T, X, G = tiles[hh]
                        handed(("m", t, n, hh))
                        by_head(("g", t, n, hh), lambda h: E[:, h, :], lambda h: T[:, h, :])
                    for hh in range(2):
                        _, _, E, T, X, G = tiles[hh]
                        wait_sp_read(pe, ("g", t, n, hh))
                        by_head(("x", t, n, hh), lambda h: G[:, h, :], lambda h: X[:, h, :])
                        if n < len(BLOCKS) - 1:
                            by_head(("t", t, n, hh), lambda h: X[:, h, :], lambda h: G[:, h, :])
                if t:
                    for hh in range(2):
                        wait_sp_read(pe, ("s", hh))
                        by_head(("ks", hh), lambda h: qkvT[:, 8 + 4 * hh + h, v], lambda h: state[:, 4 * hh + h, :])
                        by_head(("qs", hh), lambda h: qkvT[:, 4 * hh + h, v], lambda h: state[:, 4 * hh + h, :])
                for hh in range(2):
                    _, _, E, T, X, G = tiles[hh]
                    handed(("rhs", t, hh))
                    by_head(("v", t, hh), lambda h: X[:, h, :], lambda h: T[:, h, :])
                for hh in range(2):
                    Dt, G = tiles[hh][0], tiles[hh][5]
                    wait_sp_read(pe, ("v", t, hh))
                    by_head(("o", t, hh), lambda h: Dt[:, h, :], lambda h: G[:, h, :])
                    if t == 0:
                        by_head(("s", hh), lambda h: k_tok[:, 4 * hh + h, :], lambda h: G[:, h, :])
                for hh in range(2):
                    handed(("on", t, hh))
                    transposes(("y", t, hh), [tiles[hh][1][:, h, :] for h in range(4)])
            outer("out0", KT, 0)
            xT(1)
            ffn(0)
            if stop == "l0":
                return

            xT(2)
            small(S["gates"], C["gates"], 48, 2)
            for n in range(2):
                chunk(S["kcvc"] + 4 * n, C["kcvc"] + n, False)
            n_fpe = n_fp
            for b_ in range(2):
                c = C["w1"] + b_
                pe.wait_ge(pair_free[c % 2], c // 2)
                b = pair(c)[0]
                n_fpe += 1
                pe.wait_ge(for_pe, n_fpe)
                for q in range(8):
                    h = 2 * (S["w1"] + 4 * b_) + q
                    pe.wait_ge(w_lo_ready, h + 1)
                    for ll in range(4):
                        l = 4 * q + ll
                        for k in range(2):
                            cols = slice(ll * CMPH + k * P, ll * CMPH + (k + 1) * P)
                            ins = passes(b[:, 64 * k:64 * k + NCG], w_hi[:, h % HL_SLOTS, cols], w_lo[:, h % HL_SLOTS, cols],
                                         blk_hi[:, l, :], blk_lo[:, l, :], l == 0 and k == 0, l == CMPB - 1, True)
                    used(ins)
                pe.wait_ge(pair_free[c % 2], c // 2 + 1)
                if b_ == 0:
                    name = ("kcmp",)
                    b = sp_use(name)
                    for k in range(2):
                        ins = pe.matmul(b[0:NCG, 0:DH], cmp_hT[:, k, 0:NCG], w2[:, 0, k, :], start=k == 0, stop=k == 1)
                    sp_done(ins, name)
                else:
                    name = ("vcmp",)
                    b = sp_use(name)
                    for g in range(NG):
                        for k in range(2):
                            ins = pe.matmul(b[0:NCMP, g * DH:(g + 1) * DH], cmp_hT[:, k, g * NCMP:(g + 1) * NCMP],
                                            w2[:, 1, k, :], start=k == 0, stop=k == 1)
                    sp_done(ins, name)
            n_fpe += 1
            pe.wait_ge(for_pe, n_fpe)
            name = ("kcmpT",)
            b = sp_use(name)
            sp_done(pe.transpose(b[:, 0:NCG], rope_a[0:NCG, 0, 0:DH], ident[0:NCG, 0:NCG]), name)

            def heads_T(names):
                for a, name in enumerate(names):
                    b = sp_use(name)
                    for h in range(2):
                        for t in range(NT):
                            ins = pe.transpose(b[:, h * SEQ + t * P:h * SEQ + (t + 1) * P],
                                               rope_a[:, t, (2 * a + h) * P:(2 * a + h + 1) * P], ident[:, :])
                    sp_done(ins, name)

            def turned(names):
                nonlocal n_fpe
                n_fpe += 1
                pe.wait_ge(for_pe, n_fpe)
                heads_T(names)
            for b_ in range(2):
                chunk(S["kv"] + 8 * b_, C["kv"] + 2 * b_, True)
                chunk(S["kv"] + 8 * b_ + 4, C["kv"] + 2 * b_ + 1, True, between=lambda: turned([("kv", b_, a) for a in range(2)]))
            for j in range(4):
                chunk(S["q"] + 4 * j, C["q"] + j, True,
                      between=(lambda: turned([("q", 2 * j - 2 + a) for a in range(2)])) if j else None)
            turned([("q", 6 + a) for a in range(2)])

            for a in range(2):
                wait_sp_read(pe, ("q", 6 + a))
            n_fa = 16
            for g in range(NG):
                for t in range(NT):
                    v = slice(t * P, (t + 1) * P)
                    name = ("c", g, t)
                    b = sp_use(name)
                    for h in range(HPG):
                        ins = pe.matmul(b[:, h * NCMP:(h + 1) * NCMP], qT[:, 4 * g + h, v], kcmpT[:, g * NCMP:(g + 1) * NCMP], start=True, stop=True)
                    sp_done(ins, name)
                    kn = (t + 1) * P
                    hp = HPG // (t + 1)
                    for br in range(2):
                        for k in range(t + 1):
                            name = ("s", g, t, br, k)
                            b = sp_use(name)
                            for h in range(hp):
                                ins = pe.matmul(b[:, h * kn:(h + 1) * kn], qT[:, 4 * g + hp * k + h, v], ksT[:, br, g, 0:kn], start=True, stop=True)
                            sp_done(ins, name)
                    n_fpe += 1
                    pe.wait_ge(for_pe, n_fpe)
                    transposes(("cT", g, t), [sc_cmp[:, h, :] for h in range(HPG)], NCMP)
                    for br in range(2):
                        pe.wait_ge(from_act, n_fa + 2 + br)
                        for k in range(t + 1):
                            p_ = sc_buf[br][:, 0:HPG * kn].rearrange("p (h n) -> p h n", h=HPG)
                            transposes(("pT", g, t, br, k), [p_[:, h, k * P:(k + 1) * P] for h in range(HPG)])
                    n_fa += 3
                    name = ("co", g, t)
                    wait_sp_read(pe, ("cT", g, t))
                    b = sp_use(name)
                    for h in range(HPG):
                        ins = pe.matmul(b[:, h * P:(h + 1) * P], pT_cmp[0:NCMP, h * P:(h + 1) * P], vcmp[0:NCMP, g, :], start=True, stop=True)
                    sp_done(ins, name)
                    for br in range(2):
                        name = ("po", g, t, br)
                        for k in range(t + 1):
                            wait_sp_read(pe, ("pT", g, t, br, k))
                        b = sp_use(name)
                        for h in range(HPG):
                            for k in range(t + 1):
                                ins = pe.matmul(b[:, h * P:(h + 1) * P], pT_buf[br][:, k, h * P:(h + 1) * P],
                                                vs[:, br, k, g * DH:(g + 1) * DH], start=k == 0, stop=k == t)
                        sp_done(ins, name)
                    n_fpe += 1
                    pe.wait_ge(for_pe, n_fpe)
                    transposes(("oT", g, t), [o_buf[:, h, :] for h in range(HPG)])
            outer("out1", KT, 1)
            xT(3)
            ffn(1)


_INS = ['x', 'positions', 'ln_mix_g', 'ln_mix_b', 'ln_ffn_g', 'ln_ffn_b', 'ffn_w_in', 'ffn_w_out',
        'hy_w_in', 'sc_conv_w', 'dn_conv_w', 'dn_a_log', 'dn_dt_bias', 'dn_norm_w', 'hy_w_out',
        'nsa_w_in', 'cmp_pos_k', 'cmp_w1_k', 'cmp_w2_k', 'cmp_pos_v', 'cmp_w1_v', 'cmp_w2_v', 'nsa_w_out']


def kernel(**inputs):
    import concourse.bacc as bacc
    from concourse.bass_utils import run_bass_kernel_spmd as run

    nc = bacc.Bacc("TRN2", target_bir_lowering=False, num_devices=1)
    arrays, args = {}, []

    def give(name, a):
        a = np.ascontiguousarray(a)
        arrays[name] = a
        args.append(nc.dram_tensor(name, a.shape, mybir.dt.from_np(a.dtype), kind="ExternalInput").ap())

    def by_feature(a):
        a = np.asarray(a)
        return a.reshape(a.shape[0], -1, P).transpose(2, 1, 0)

    laid = dict(inputs)
    for name in ("sc_conv_w", "dn_conv_w"):
        laid[name] = by_feature(inputs[name][0]).reshape(P, -1)
    for name in ("cmp_pos_k", "cmp_pos_v"):
        laid[name] = np.asarray(inputs[name])[0].T
    for name in _INS:
        give(f"in_{name}_dram", laid[name])
    half = DH // 2
    give("inv_freq_dram", np.power(np.float32(10000.0), -np.arange(half, dtype=np.float32) / half).astype(np.float32))
    norms = [(inputs[f"ln_{k}_g"][i], inputs[f"ln_{k}_b"][i]) for i in range(DEPTH) for k in ("mix", "ffn")]
    give("ln_by_feature_dram", np.stack([np.stack([np.asarray(v).reshape(KT, P).T for v in n], 1) for n in norms], 1))
    give("end_positions_dram", np.tile(np.asarray(inputs["positions"])[0, CMPB - 1::STRIDE], NG).reshape(NCG, 1))
    args.append(nc.dram_tensor("out_dram", (1, SEQ, D), F32, kind="ExternalOutput").ap())
    trunk(nc, *args, stop=STOP)
    r = run(nc, [arrays], core_ids=[0])
    return r.results[0]["out_dram"]
```

```python
from contextlib import ExitStack

import numpy as np
import concourse.bass as bass
from concourse import mybir

F32 = mybir.dt.float32
F32R = mybir.dt.float32r
I32 = mybir.dt.int32
ALU = mybir.AluOpType
ACT = mybir.ActivationFunctionType
AX = mybir.AxisListType
ds = bass.ds

P = 128
D = 2048
KT = D // P
SEQ = 256
NT = SEQ // P
DEPTH = 2
FFN = ((8 * D + 3 * 256 - 1) // (3 * 256)) * 256
FT = FFN // P
CH = 512
SC = D // 2
SCK, DNK = 3, 4
DNH = 8
NH, NG = 16, 4
HPG = NH // NG
DH = 128
CMPB, STRIDE = 32, 16
NCMP = SEQ // STRIDE - CMPB // STRIDE + 1
NCG = NCMP * NG
CMPH = 2 * DH
ALPHA = (2 * DEPTH) ** 0.25
LN_EPS, NORM_EPS = 1e-5, 1e-6
NEG = -1e30
SCALE = DH ** -0.5
TWO_PI_1 = 6.28125
TWO_PI_2 = float(np.float32(2 * np.pi - 6.28125))
TWO_PI_3 = float(2 * np.pi - 6.28125 - TWO_PI_2)
PI = 3.1415925
ROUND = 1.5 * 2.0 ** 23

RAW_SLOTS, HL_SLOTS = 4, 4
STOP = None
BLOCKS = (1, 2, 4, 8, 16, 32, 64)


def at(c, i=None, per=0):
    return c if i is None else i * per + c


class Plan:

    def __init__(self):
        self.slab, self.chunk = {}, {}
        s = c = 0
        for name, slabs, chunks in (
            ("z0", 4, 1), ("ba", 1, 1), ("z1", 4, 1), ("qkv", 24, 6), ("sc", 24, 6), ("out0", 16, 0),
            ("ffn0", 88, 22), ("fout0", FT, 0),
            ("kc", 4, 1), ("gates", 1, 1), ("vc", 4, 1), ("w1", 8, 2), ("kv", 16, 4), ("q", 16, 4), ("out1", 16, 0),
            ("ffn1", 88, 22), ("fout1", FT, 0),
        ):
            self.slab[name], self.chunk[name] = s, c
            s, c = s + slabs, c + chunks


def trunk(nc, x_in, positions, ln_mix_g, ln_mix_b, ln_ffn_g, ln_ffn_b, ffn_w_in, ffn_w_out,
          hy_w_in, sc_conv_w, dn_conv_w, dn_a_log, dn_dt_bias, dn_norm_w, hy_w_out,
          nsa_w_in, cmp_pos_k, cmp_w1_k, cmp_w2_k, cmp_pos_v, cmp_w1_v, cmp_w2_v, nsa_w_out,
          inv_freq, ln_by_feature, end_positions, out, stop=None):
    plan = Plan()
    S, C = plan.slab, plan.chunk
    ctx = ExitStack()
    with ctx:
        def sem(name):
            return ctx.enter_context(nc.semaphore(name))

        place = [16512]

        def sb(name, shape, dt=F32, offset=None):
            size = 4 * int(np.prod(shape[1:]))
            if offset is None:
                offset = place[0]
                place[0] += (size + 31) // 32 * 32
            return nc.alloc_sbuf_tensor_at(name, shape, dt, offset=offset)

        raw = sb("raw", [P, RAW_SLOTS, 2048])
        w_hi = sb("w_hi", [P, HL_SLOTS, 1024], F32R)
        w_lo = sb("w_lo", [P, HL_SLOTS, 1024], F32R)
        xt_at = place[0]
        xt_hi = sb("xt_hi", [P, KT, SEQ], F32R)
        xt_lo = sb("xt_lo", [P, KT, SEQ], F32R)
        x = sb("x", [P, NT, D])
        a_hi = sb("a_hi", [P, 4, SEQ], F32R)
        a_lo = sb("a_lo", [P, 4, SEQ], F32R)
        big_at = place[0]
        big = sb("big", [P, 12288])
        yt = sb("yt", [P, KT, SEQ])
        gb_at = place[0]
        gb = sb("gb", [P, 2, D])
        ident = sb("ident", [P, P])
        ones = sb("ones", [P, P])
        upper = sb("upper", [P, P])
        neg_lower = sb("neg_lower", [P, P])
        blk_mask = sb("blk_mask", [P, len(BLOCKS), P])
        lnT = sb("lnT", [P, 2, KT])
        stats = sb("stats", [P, NT, 4, 6])
        mv = sb("mv", [P, NT, 2])
        rstd = sb("rstd", [P, NT])
        nmr = sb("nmr", [P, NT])
        eps_ln = sb("eps_ln", [P, 1])
        eps_nm = sb("eps_nm", [P, 1])
        half_pi = sb("half_pi", [P, 1])
        sm = sb("sm", [P, 16, 16])
        misc_w = sb("misc_w", [P, 136])

        used = 0

        def part(n, shape_str=None, **kw):
            nonlocal used
            v = big[:, used:used + n]
            used += n
            assert used <= 12288
            return v.rearrange(shape_str, **kw) if shape_str else v

        qkvT = part(24 * SEQ, "p (f t) -> p f t", f=24)
        k_tok = part(1024, "p (h d) -> p h d", h=DNH)
        state = part(1024, "p (h d) -> p h d", h=DNH)
        norm_w = state[:, 0, :]
        v_tok = part(2048, "p (t h d) -> p t h d", t=NT, h=DNH)
        z_tok = part(2048, "p (t h d) -> p t h d", t=NT, h=DNH)
        vT = qkvT[:, 16:24, :]
        vT_flat = big[:, 16 * SEQ:24 * SEQ]
        gb_flat = gb[:, :, :].rearrange("p a n -> p (a n)")

        def dn_tile(n):
            base, m = (gb_flat, n) if n < 8 else (vT_flat, n - 8)
            return base[:, m * 512:(m + 1) * 512].rearrange("p (h d) -> p h d", h=4)
        dn_more = sb("dn_more", [P, 12, 512], offset=xt_at)

        def tiles_of(t, hh):
            if t == 0:
                return [dn_tile(6 * hh + n) for n in range(6)]
            return [dn_more[:, 6 * hh + n, :].rearrange("p (h d) -> p h d", h=4) for n in range(6)]
        units = [(t, hh) for t in range(NT) for hh in range(2)]
        conv_in = gb_flat[:, 0:2048].rearrange("p (a f t) -> p a f t", a=2, f=4)
        conv_out = gb_flat[:, 2048:3072].rearrange("p (f t) -> p f t", f=4)
        ba_out = gb_flat[:, 0:SEQ]
        norm_sq, norm_q = dn_tile(6), dn_tile(7)
        hT = big[:, 0:FT * SEQ].rearrange("p (f t) -> p f t", f=FT)
        yt_flat = yt[:, :, :].rearrange("p a t -> p (a t)")
        sg = yt_flat[:, 0:1024].rearrange("p (t n) -> p t n", t=NT)
        hid = yt_flat[:, 1024:2048].rearrange("p (t n) -> p t n", t=NT)
        used = 0
        qT = part(NH * SEQ, "p (h t) -> p h t", h=NH)
        ksT = part(2 * NG * SEQ, "p (b h t) -> p b h t", b=2, h=NG)
        gates_out = ksT[:, 0, 0, :]
        vs = part(2 * NT * 512, "p (b t n) -> p b t n", b=2, t=NT)
        kcT = part(2 * NG * SEQ, "p (b h t) -> p b h t", b=2, h=NG)
        kcmpT = part(64)
        vcmp = part(NG * DH, "p (g d) -> p g d", g=NG)
        w2 = part(2 * 2 * DH, "p (b k n) -> p b k n", b=2, k=2)
        neg_cmp = part(NT * NCMP, "p (t n) -> p t n", t=NT)
        ok_cmp = part(NT * NCMP, "p (t n) -> p t n", t=NT)
        cmp_h = yt_flat[:, 3840:3840 + CMPH]
        cmp_hT = part(128, "p (k n) -> p k n", k=2)
        neg_upper = part(2 * P, "p (a n) -> p a n", a=2)
        posT = part(2 * CMPB, "p (b l) -> p b l", b=2)
        rope_in = yt_flat[:, 0:1024].rearrange("p (t n) -> p t n", t=NT)
        rope_a = yt_flat[:, 1024:2048].rearrange("p (t n) -> p t n", t=NT)
        rope_b = yt_flat[:, 2048:3072].rearrange("p (t n) -> p t n", t=NT)
        cosb = yt_flat[:, 3072:3328].rearrange("p (t n) -> p t n", t=NT)
        sinb = yt_flat[:, 3328:3584].rearrange("p (t n) -> p t n", t=NT)
        cosc = yt_flat[:, 3584:3712]
        sinc = yt_flat[:, 3712:3840]
        blk_sum = yt_flat[:, 0:CMPB * NCG].rearrange("p (l r) -> p l r", l=CMPB)
        angle = yt_flat[:, 2048:2240].rearrange("p (a n) -> p a n", a=3)
        turns = yt_flat[:, 2240:2432].rearrange("p (a n) -> p a n", a=3)
        sc_buf = [gb_flat[:, 1024 * n:1024 * n + 1024] for n in range(2)]
        pT_buf = [gb_flat[:, 2048 + 1024 * n:3072 + 1024 * n].rearrange("p (k m) -> p k m", k=2) for n in range(2)]
        kc_flat = kcT.rearrange("p b h t -> p (b h t)")
        o_buf = kc_flat[:, 0:512].rearrange("p (h d) -> p h d", h=HPG)
        sc_cmp = kc_flat[:, 512:512 + HPG * NCMP].rearrange("p (h n) -> p h n", h=HPG)
        pT_cmp = kc_flat[:, 640:1152]
        gates = sm[:, 8:14, :].rearrange("p a b -> p (a b)").rearrange("p (t n) -> p t n", t=NT)
        blk_n, blk_w = CMPB * NCG, CMPB * NCG + P - NCG
        blk_at = (gb_at, big_at)
        blk_hi = [sb(f"blk_hi{b}", [P, blk_w], F32R, offset=blk_at[b]) for b in range(2)]
        blk_lo = [sb(f"blk_lo{b}", [P, blk_w], F32R, offset=blk_at[b] + 4 * D) for b in range(2)]

        bank = [ctx.enter_context(nc.psum_tensor(f"bank{n}", [P, 512], F32)) for n in range(8)]

        def pair(c):
            return bank[2 * (c % 2)], bank[2 * (c % 2) + 1]

        slab_in = [sem(f"slab_in{n}") for n in range(RAW_SLOTS)]
        w_hi_ready, w_lo_ready = sem("w_hi_ready"), sem("w_lo_ready")
        half_used = sem("half_used")
        a_hi_ready, a_lo_ready = sem("a_hi_ready"), sem("a_lo_ready")
        pair_free = [sem(f"pair_free{n}") for n in range(2)]
        sp_ready = [sem(f"sp_ready{n}") for n in range(4)]
        sp_free = [sem(f"sp_free{n}") for n in range(4)]
        x_in_sem, small_in, nsa_in, w2_in = sem("x_in_sem"), sem("small_in"), sem("nsa_in"), sem("w2_in")
        gb_in, out_done = sem("gb_in"), sem("out_done")
        consts, pool_chain, x_scaled = sem("consts"), sem("pool_chain"), sem("x_scaled")
        dve, act_done = sem("dve"), sem("act_done")
        var_ready, std_ready, nmr_ready, x_normed = sem("var_ready"), sem("std_ready"), sem("nmr_ready"), sem("x_normed")
        xt_hi_ready, xt_lo_ready = sem("xt_hi_ready"), sem("xt_lo_ready")
        stage_free, silu_done = sem("stage_free"), sem("silu_done")
        hid_ready = sem("hid_ready")
        first_whole = sem("first_whole")
        ident_ready, out_ready = sem("ident_ready"), sem("out_ready")
        for_act, for_pe, from_act, gb_free = sem("for_act"), sem("for_pe"), sem("from_act"), sem("gb_free")

        block = ctx.enter_context(nc.Block())

        def pair(c):
            return bank[2 * (c % 2)], bank[2 * (c % 2) + 1]

        K, n_uses = {}, 0

        def uses(names):
            nonlocal n_uses
            for name in names:
                K[name] = n_uses
                n_uses += 1

        uses([("xT", 0, u) for u in range(8)])
        uses([("ba",)])
        uses([("norm", u) for u in range(8)])
        uses([("gc",)])
        uses([("ktok", hh) for hh in range(2)] + [("vtok", t, hh) for t in range(NT) for hh in range(2)])
        for t, hh in units:
            uses([("row", t, hh), ("beta", t, hh), ("kk", t, hh), ("kq", t, hh)])
        uses([("eT", t, hh) for t, hh in units])
        for n in range(1, len(BLOCKS)):
            uses([("g", t, n, hh) for t, hh in units])
            for t, hh in units:
                uses([("x", t, n, hh)] + [("t", t, n, hh)] * (n < len(BLOCKS) - 1))
        for t in range(NT):
            if t:
                for hh in range(2):
                    uses([("ks", hh), ("qs", hh)])
            uses([("v", t, hh) for hh in range(2)])
            for hh in range(2):
                uses([("o", t, hh)] + [("s", hh)] * (t == 0))
            uses([("y", t, hh) for hh in range(2)])
        uses([("xT", 1, u) for u in range(8)])
        uses([("ffn", 0, n) for n in range(2 * FFN // CH)])
        uses([("xT", 2, u) for u in range(8)])
        uses([("gates",), ("kh",), ("kcmp",), ("kcmpT",), ("vh",), ("vcmp",)])
        uses([("kv", b, a) for b in range(2) for a in range(2)])
        for g in range(NG):
            uses([("q", 2 * g + a) for a in range(2)])
            for t in range(NT):
                uses([("c", g, t)] + [("s", g, t, b, k) for b in range(2) for k in range(t + 1)])
                uses([("cT", g, t)] + [("pT", g, t, b, k) for b in range(2) for k in range(t + 1)])
                uses([("co", g, t)] + [("po", g, t, b) for b in range(2)] + [("oT", g, t)])
        uses([("xT", 3, u) for u in range(8)])
        uses([("ffn", 1, n) for n in range(2 * FFN // CH)])

        def sp_bank(name):
            return bank[4 + K[name] % 4]

        def wait_sp(eng, name, i=None, per=0):
            eng.wait_ge(sp_ready[K[name] % 4], at(K[name] // 4 + 1, i, per // 4))

        def wait_sp_read(eng, name):
            eng.wait_ge(sp_free[K[name] % 4], K[name] // 4 + 1)

        chunk_end = {}
        for name, m in (("ba", 0), ("z0", 1), ("z1", 1), ("qkv", 6), ("sc", 6), ("ffn0", 22), ("gates", 0), ("kc", 1), ("vc", 1), ("w1", 2),
                        ("kv", 4), ("q", 4), ("ffn1", 22)):
            for n in range(m or 1):
                chunk_end[C[name] + n] = 2 * S[name] + (8 * (n + 1) if m else 2)

        FP, n_fp = {}, 0

        def hands(names):
            nonlocal n_fp
            for name in names:
                n_fp += 1
                FP[name] = n_fp

        hands([("g",)])
        hands([("rows", t, hh) for t, hh in units])
        for n in range(len(BLOCKS)):
            hands([("m", t, n, hh) for t, hh in units])
        for t in range(NT):
            hands([("rhs", t, hh) for hh in range(2)])
            hands([("on", t, hh) for hh in range(2)])

        @block.sync
        def _(sp):
            def slab(s, src, view, i=None, per=0):
                if s >= RAW_SLOTS:
                    sp.wait_ge(w_lo_ready, at(2 * (s - RAW_SLOTS) + 2, i, 2 * per))
                sp.dma_start(view(raw[:, s % RAW_SLOTS, :]), src).then_inc(slab_in[s % RAW_SLOTS], 16)

            def as_in(v):
                return v.rearrange("p (k n) -> p k n", k=4)

            def cols(w, quad, col):
                return w[quad * 512:(quad + 1) * 512, col].rearrange("(k p) n -> p k n", p=P)

            def small(name, w):
                lo = w.shape[-1] - P
                slab(S[name], w[:, lo:lo + P].rearrange("(k p) n -> p k n", p=P),
                     lambda v: v.rearrange("p (k n) -> p k n", k=KT))

            def chunk(s, w, col, i=None, per=0):
                for quad in range(4):
                    slab(s + quad, cols(w, quad, col), as_in, i, per)

            def outer(name, w, n):
                with sp.Fori(0, n // 4) as i:
                    for j in range(4):
                        slab(S[name] + j, w[ds(i * 512 + j * P, P), :], lambda v: v, i, 4)

            def ffn(name, layer):
                w = ffn_w_in[layer]
                for j in range(2):
                    chunk(S[name] + 4 * j, w, slice(j * FFN, j * FFN + CH))
                with sp.Fori(0, 5) as i:
                    for n in range(4):
                        chunk(S[name] + 8 + 4 * n, w, ds(i * 2 * CH + (n // 2 + 1) * CH + (n % 2) * FFN, CH), i, 16)
                outer("fout" + name[-1], ffn_w_out[layer], FT)

            for t in range(NT):
                sp.dma_start(x[:, t, :], x_in[0, t * P:(t + 1) * P, :]).then_inc(x_in_sem, 16)
            w = hy_w_in[0]
            for j in range(2):
                chunk(S[f"z{j}"], w, slice(6144 + j * CH, 6144 + (j + 1) * CH))
                if j == 0:
                    small("ba", w)
            with sp.Fori(0, 3) as i:
                for j in range(2):
                    chunk(S["qkv"] + 4 * j, w, ds(i * 2 * CH + 3 * SC + j * CH, CH), i, 8)
            for j in range(2):
                for n, lo in enumerate((SC, 2 * SC, 0)):
                    chunk(S["sc"] + 12 * j + 4 * n, w, slice(lo + j * CH, lo + (j + 1) * CH))
            outer("out0", hy_w_out[0], KT)
            ffn("ffn0", 0)
            if stop != "l0":
                w = nsa_w_in[0]
                for b, name in enumerate(("kc", "vc")):
                    chunk(S[name], w, slice(2048 + b * CH, 2048 + (b + 1) * CH))
                    if b == 0:
                        small("gates", w)
                for b, w1 in enumerate((cmp_w1_k, cmp_w1_v)):
                    for q in range(4):
                        slab(S["w1"] + 4 * b + q, w1[0][q * 1024:(q + 1) * 1024, :].rearrange("(l p) n -> p l n", p=P),
                             lambda v: v.rearrange("p (l n) -> p l n", l=8))
                for n in range(4):
                    chunk(S["kv"] + 4 * n, w, slice(3072 + n * CH, 3072 + (n + 1) * CH))
                for j in range(4):
                    chunk(S["q"] + 4 * j, w, slice(j * CH, (j + 1) * CH))
                outer("out1", nsa_w_out[0], KT)
                ffn("ffn1", 1)
            for n in range(2 * NT):
                sp.wait_ge(out_ready, n + 1)
                rows, col = slice(n // 2 * P, (n // 2 + 1) * P), slice(n % 2 * D // 2, (n % 2 + 1) * D // 2)
                sp.dma_start(out[0, rows, col], x[:, n // 2, col]).then_inc(out_done, 16)
            sp.wait_ge(out_done, 16 * 2 * NT)

        @block.gpsimd
        def _(pool):
            def bcast(ap, n):
                return ap.rearrange("(a n) -> a n", a=1).to_broadcast([P, n])

            count = [0]

            def own(ins):
                count[0] += 1
                ins.then_inc(pool_chain, 1)
                pool.wait_ge(pool_chain, count[0])

            def select(ap, pattern, base, mult, fill):
                own(pool.affine_select(out=ap, in_=ap, pattern=pattern, compare_op=ALU.is_ge, fill=fill,
                                       base=base, channel_multiplier=mult))

            own(pool.memset(ident[:, :], 0.0))
            pool.affine_select(out=ident[:, :], in_=ident[:, :], pattern=[[-1, P]], compare_op=ALU.not_equal, fill=1.0,
                               base=0, channel_multiplier=1).then_inc(ident_ready, 1)
            for m, v in ((ones, 1.0), (upper, 1.0), (neg_lower, 0.0), (blk_mask, 0.0)):
                own(pool.memset(m[:, :] if len(m.shape) == 2 else m[:, :, :], v))
            select(upper[:, :], [[1, P]], 0, -1, 0.0)
            select(neg_lower[:, :], [[1, P]], 0, -1, NEG)
            for n, b in enumerate(BLOCKS):
                v = blk_mask[:, n, :].rearrange("p (m a r) -> p m a r", a=2, r=b)[:, :, 1, :]
                own(pool.memset(v, 1.0))
                select(v, [[-2 * b, P // (2 * b)], [0, b]], 0, 1, 0.0)
                select(v, [[2 * b, P // (2 * b)], [0, b]], b - 1, -1, 0.0)
            pool.memset(eps_ln[:, :], LN_EPS).then_inc(consts, 1)
            pool.memset(eps_nm[:, :], NORM_EPS).then_inc(consts, 1)
            pool.memset(half_pi[:, :], float(np.pi / 2)).then_inc(consts, 1)
            pool.dma_start(misc_w[:, 0:96], dn_conv_w).then_inc(small_in, 16)
            pool.dma_start(misc_w[:, 96:120], sc_conv_w).then_inc(small_in, 16)
            pool.dma_start(norm_w, bcast(dn_norm_w[0], DH)).then_inc(small_in, 16)
            pool.dma_start(misc_w[:, 120:128], bcast(dn_a_log[0], DNH)).then_inc(small_in, 16)
            pool.dma_start(misc_w[:, 128:136], bcast(dn_dt_bias[0], DNH)).then_inc(small_in, 16)

            def layer_norm(n, g, b):
                pool.wait_ge(gb_free, n + 1)
                if n:
                    pool.wait_ge(x_scaled, NT * n)
                for a, v in enumerate((g, b)):
                    pool.dma_start(gb[:, a, :], bcast(v, D)).then_inc(gb_in, 16)
                pool.dma_start(lnT[:, :, :], ln_by_feature[:, n, :, :]).then_inc(gb_in, 16)
                pool.wait_ge(gb_in, 48 * (n + 1))
                last = 2 * DEPTH - 1 if stop != "l0" else 1
                if n < last:
                    for bk in range(4):
                        wait_sp(pool, ("xT", n + 1, 4 + bk))
                else:
                    return
                for t in range(NT):
                    own(pool.tensor_tensor(x[:, t, :], x[:, t, :], gb[:, 0, :], ALU.mult))
                    pool.tensor_tensor(x[:, t, :], x[:, t, :], gb[:, 1, :], ALU.add).then_inc(x_scaled, 1)

            layer_norm(0, ln_mix_g[0], ln_mix_b[0])
            if stop != "l0":
                for t in range(NT):
                    for m, v, fill in ((neg_cmp, 0.0, NEG), (ok_cmp, 1.0, 0.0)):
                        own(pool.memset(m[:, t, :], v))
                        select(m[:, t, :], [[-STRIDE, NCMP]], t * P - (CMPB - 1), 1, fill)
                own(pool.memset(neg_upper, 0.0))
                select(neg_upper[:, 1, :], [[-1, P]], 0, 1, NEG)
                for t in range(NT):
                    pool.dma_start(misc_w[:, 64 + t:65 + t].bitcast(I32), positions[0][t * P:(t + 1) * P].rearrange("(p a) -> p a", a=1)).then_inc(nsa_in, 16)
                pool.dma_start(misc_w[0:NCG, 66:67].bitcast(I32), end_positions).then_inc(nsa_in, 16)
                pool.dma_start(misc_w[:, 0:64], bcast(inv_freq, DH // 2)).then_inc(nsa_in, 16)
                for b, p in enumerate((cmp_pos_k, cmp_pos_v)):
                    pool.dma_start(posT[:, b, :], p).then_inc(nsa_in, 16)
            layer_norm(1, ln_ffn_g[0], ln_ffn_b[0])
            if stop != "l0":
                for b, w in enumerate((cmp_w2_k, cmp_w2_v)):
                    pool.dma_start(w2[:, b, :, :], w[0].rearrange("(k p) n -> p k n", p=P)).then_inc(w2_in, 16)
                layer_norm(2, ln_mix_g[1], ln_mix_b[1])
                layer_norm(3, ln_ffn_g[1], ln_ffn_b[1])

        total_slabs = S["kc"] if stop == "l0" else S["fout1"] + FT
        LEAD = 3
        A0 = {"out0": 0, "fout0": KT, "out1": KT + FT, "fout1": 2 * KT + FT}

        def half_of(h):
            return raw[:, h // 2 % RAW_SLOTS, h % 2 * 1024:h % 2 * 1024 + 1024], h % HL_SLOTS

        def outer_src(name):
            return hT if name[0] == "f" else qT if name == "out1" else yt

        @block.scalar
        def _(act):
            h_next = [0]

            def halves(count, i=None, per=0):
                for _ in range(count):
                    h = h_next[0]
                    if h >= 2 * total_slabs:
                        return
                    src, slot = half_of(h)
                    if h % 2 == 0:
                        act.wait_ge(slab_in[h // 2 % RAW_SLOTS], at(16 * (h // 2 // RAW_SLOTS + 1), i, 2 * per))
                    if h >= HL_SLOTS:
                        act.wait_ge(half_used, at(h - HL_SLOTS + 1, i, per))
                    act.activation(w_hi[:, slot, :], src, ACT.Copy).then_inc(w_hi_ready, 1)
                    h_next[0] += 1

            def loop_over(n, per_halves, body):
                with act.Fori(0, n) as i:
                    body(i)
                h_next[0] += (n - 1) * per_halves

            def chunk_in(c, i=None, per=0):
                act.wait_ge(half_used, at(chunk_end[c], i, 16 * per))
                return pair(c)

            def split_xt(m):
                for q in range(4):
                    if m == 0:
                        for u in (2 * q, 2 * q + 1):
                            wait_sp(act, ("xT", m, u))
                            ins = act.activation(xt_hi[:, 2 * u:2 * u + 2, :], sp_bank(("xT", m, u))[:, :].rearrange("p (a t) -> p a t", a=2),
                                                 ACT.Copy)
                        ins.then_inc(xt_hi_ready, 1)
                        continue
                    for u in (2 * q, 2 * q + 1):
                        wait_sp_read(act, ("xT", m, u))
                    act.activation(xt_hi[:, 4 * q:4 * q + 4, :], yt[:, 4 * q:4 * q + 4, :], ACT.Copy).then_inc(xt_hi_ready, 1)
                    if q < LEAD - 1:
                        halves(1)

            def outer(name, n):
                src = outer_src(name)

                def split(kt, i=None):
                    act.wait_ge(half_used, at(2 * (S[name] + kt) - 6, i, 8))
                    col = kt if i is None else ds(i * 4 + kt, 1)
                    s_ = src[:, col, :]
                    act.activation(a_hi[:, kt % 4, :], s_, ACT.Copy).then_inc(a_hi_ready, 1)

                def quad(kt, i=None):
                    for j in range(4):
                        if kt + j + 1 < n:
                            split(kt + j + 1, i)
                        halves(2 if kt + j < n - 2 or i is not None else n - 1 - kt - j, i, 8)
                split(0)
                loop_over(n // 4 - 1, 8, lambda i: quad(0, i))
                quad(n - 4)

            def ln(n, last=False):
                def normalise(t):
                    act.wait_ge(nmr_ready, NT * n + t + 1)
                    m = 4 if t else 1
                    for c in range(m):
                        if c == 2:
                            halves(1)
                        v = x[:, t, c * D // m:(c + 1) * D // m]
                        act.activation(v, v, ACT.Identity, bias=nmr[:, t:t + 1], scale=rstd[:, t:t + 1]).then_inc(x_normed, 1)

                for t in range(NT):
                    act.wait_ge(var_ready, NT * n + t + 1)
                    act.activation(rstd[:, t:t + 1], mv[:, t, 1:2], ACT.Sqrt, bias=eps_ln[:, :]).then_inc(std_ready, 1)
                    if t == 0 and not last:
                        normalise(0)
                if not last:
                    normalise(1)

            def ffn(layer):
                c0, k0 = C[f"ffn{layer}"], K[("ffn", layer, 0)]
                n_sg = layer * (FFN // CH)

                def gate(c, n, i=None):
                    b = chunk_in(c, i, 2)
                    if n_sg + n > 0:
                        act.wait_ge(hid_ready, at(n_sg + n, i, 2))
                    for t in range(NT):
                        ins = act.activation(sg[:, t, :], b[t][:, :], ACT.Silu)
                    ins.then_inc(pair_free[c % 2], 1)

                def put_hT(k, f, i=None):
                    for a in range(2):
                        act.wait_ge(sp_ready[(k + a) % 4], at((k + a) // 4 + 1, i, 1))
                        col = slice(f + 2 * a, f + 2 * a + 2) if i is None else ds(i * 8 + f + 2 * a, 2)
                        dst = hT[:, col, :]
                        act.activation(dst, bank[4 + (k + a) % 4][:, :].rearrange("p (a t) -> p a t", a=2),
                                       ACT.Copy).then_inc(sp_free[(k + a) % 4], 1)

                halves(8)
                gate(c0, 0)
                halves(8)

                def body(i):
                    for n in range(2):
                        halves(8, i, 32)
                        gate(c0 + 2 + 2 * n, 1 + n, i)
                        put_hT(k0 + 2 * n, 4 * n, i)
                        halves(8, i, 32)
                loop_over(5, 32, body)
                put_hT(k0 + 20, 40)
                for a in range(2):
                    act.wait_ge(sp_free[(k0 + 20 + a) % 4], (k0 + 20 + a) // 4 + 1)
                outer(f"fout{layer}", FT)

            def last_cols(name, n):
                return sp_bank(name)[:, 0:SEQ].rearrange("p (t m) -> p t m", t=NT)[:, :, P - n:]

            halves(LEAD)
            split_xt(0)
            for j in range(2):
                if j:
                    halves(2)
                    c = C["ba"]
                    act.activation(ba_out, chunk_in(c)[0][:, 0:SEQ], ACT.Copy).then_inc(pair_free[c % 2], 1)
                halves(8)
                if j:
                    wait_sp(act, ("ba",))
                    act.activation(sm[:, 0:NT, :], last_cols(("ba",), 2 * DNH), ACT.Copy).then_inc(sp_free[K[("ba",)] % 4], 1)
                c = C[f"z{j}"]
                b = chunk_in(c)
                for t in range(NT):
                    ins = act.activation(z_tok[:, t, 4 * j:4 * j + 4, :], b[t][:, :].rearrange("p (h d) -> p h d", h=4), ACT.Silu)
                ins.then_inc(pair_free[c % 2], 1)

            def qkv_turn(i):
                for j in range(2):
                    halves(8, i, 16)
                    c = C["qkv"] + j
                    b = chunk_in(c, i, 1)
                    act.wait_ge(stage_free, at(j + 1, i, 2))
                    for n in range(2):
                        ins = act.activation(conv_in[:, j, 2 * n:2 * n + 2, :],
                                             b[n][:, :].rearrange("p (f t) -> p f t", f=2), ACT.Copy)
                    ins.then_inc(pair_free[c % 2], 1)
            loop_over(3, 16, qkv_turn)
            n_from = [0]

            def done(ins):
                n_from[0] += 1
                ins.then_inc(from_act, 1)

            def square(u):
                act.activation(norm_sq, qkvT[:, 2 * u:2 * u + 2, :].rearrange("p f (a t) -> p (f a) t", a=2),
                               ACT.Square).then_inc(act_done, 1)

            def norm(u):
                wait_sp(act, ("norm", u))
                if u:
                    act.wait_ge(for_act, u)
                act.activation(norm_q, sp_bank(("norm", u))[:, :].rearrange("p (h d) -> p h d", h=4),
                               ACT.Sqrt, bias=eps_nm[:, :]).then_inc(sp_free[K[("norm", u)] % 4], 1)

            act.wait_ge(consts, 3)
            soft, expA = sm[:, 9, :], misc_w[:, 120:128]
            for j in range(2):
                for n in range(3):
                    m = 3 * j + n
                    if m == 0:
                        halves(8)
                    elif m < 5:
                        act.wait_ge(silu_done, m)
                        square(2 * m - 2)
                        halves(4)
                        norm(2 * m - 2)
                        square(2 * m - 1)
                        halves(3)
                        norm(2 * m - 1)
                        halves(1)
                    else:
                        halves(3)
                        act.wait_ge(for_act, 9)
                        done(act.activation(soft, sm[:, 8, :], ACT.Exp, scale=-1.0))
                        act.wait_ge(from_act, n_from[0])
                        done(act.activation(soft, soft, ACT.Ln, bias=1.0))
                        done(act.activation(expA, expA, ACT.Exp))
                        halves(5)
                    if n == 0:
                        c = C["sc"] + 3 * j
                        b = chunk_in(c)
                        act.wait_ge(stage_free, 7 + j)
                        for a in range(2):
                            ins = act.activation(conv_in[:, j, 2 * a:2 * a + 2, :],
                                                 b[a][:, :].rearrange("p (f t) -> p f t", f=2), ACT.Copy)
                        ins.then_inc(pair_free[c % 2], 1)
                    act.wait_ge(stage_free, m + 3)
                    act.activation(qkvT[:, 4 * m:4 * m + 4, :], qkvT[:, 4 * m:4 * m + 4, :], ACT.Silu).then_inc(silu_done, 1)

            act.wait_ge(for_act, 10)
            done(act.activation(sm[:, 6, :], sm[:, 4, :], ACT.Exp))
            done(act.activation(sm[:, 14, 8:16], sm[:, 14, 8:16], ACT.Exp))
            wait_sp_read(act, ("ba",))
            done(act.activation(sm[:, 2, :].rearrange("p (t h) -> p t h", t=NT), sm[:, 0:2, 0:8], ACT.Sigmoid))

            def put(name, dst, n=512):
                wait_sp(act, name)
                act.activation(dst, sp_bank(name)[:, 0:n].rearrange("p (h d) -> p h d", h=4), ACT.Copy)\
                   .then_inc(sp_free[K[name] % 4], 1)

            for hh in range(2):
                put(("ktok", hh), k_tok[:, 4 * hh:4 * hh + 4, :])
            for t in range(NT):
                for hh in range(2):
                    put(("vtok", t, hh), v_tok[:, t, 4 * hh:4 * hh + 4, :])
            n_ss = 10
            for t, hh in units:
                wait_sp_read(act, ("row", t, hh))
                dt_ = tiles_of(t, hh)[0]
                done(act.activation(dt_, dt_, ACT.Exp))
            for n in range(1, len(BLOCKS)):
                for t, hh in units:
                    put(("g", t, n, hh), tiles_of(t, hh)[5])
            for t in range(NT):
                for hh in range(2):
                    put(("v", t, hh), tiles_of(t, hh)[5])
                for hh in range(2):
                    n_ss += 1
                    act.wait_ge(for_act, n_ss)
                    done(act.activation(sm[:, 11, 4 * hh:4 * hh + 4], sm[:, 10, 4 * hh:4 * hh + 4], ACT.Sqrt,
                                        bias=eps_nm[:, :], scale=1.0 / DH))
                for hh in range(2):
                    put(("y", t, hh), yt[:, 8 + 4 * hh:12 + 4 * hh, t * P:(t + 1) * P])
            for hh in range(2):
                wait_sp_read(act, ("y", 1, hh))
            outer("out0", KT)
            ln(0)
            split_xt(1)
            ffn(0)
            ln(1, stop == "l0")
            if stop == "l0":
                return

            def rotary_tables():
                act.wait_ge(for_act, 15)
                for r, n in ((slice(0, P), slice(0, 2)), (slice(0, NCG), slice(2, 3))):
                    m = 2 if n.start == 0 else 1
                    half_n = DH // 2
                    sv = sinb[r] if m == 2 else sinc[r].rearrange("p (t n) -> p t n", t=1)
                    cv = cosb[r] if m == 2 else cosc[r].rearrange("p (t n) -> p t n", t=1)
                    act.activation(sv[:, :, half_n:], angle[r, n, :], ACT.Sin)
                    done(act.activation(cv[:, :, half_n:], turns[r, n, :], ACT.Sin, bias=half_pi[r], scale=-1.0))

            split_xt(2)
            for n, kv in enumerate(("kc", "vc")):
                if n:
                    halves(2)
                    c = C["gates"]
                    act.activation(gates_out, chunk_in(c)[0][:, 0:SEQ], ACT.Copy).then_inc(pair_free[c % 2], 1)
                halves(8)
                if n:
                    wait_sp(act, ("gates",))
                    act.activation(gates, last_cols(("gates",), 3 * NH), ACT.Sigmoid).then_inc(sp_free[K[("gates",)] % 4], 1)
                c = C[kv]
                b = chunk_in(c)
                for a in range(2):
                    ins = act.activation(kcT[:, n, 2 * a:2 * a + 2, :], b[a][:, :].rearrange("p (f t) -> p f t", f=2), ACT.Copy)
                ins.then_inc(pair_free[c % 2], 1)
                if n == 0:
                    rotary_tables()

            def put_hT(name):
                wait_sp(act, name)
                act.activation(cmp_hT[:, :, 0:NCG], sp_bank(name)[:, 0:128].rearrange("p (k n) -> p k n", k=2)[:, :, 0:NCG],
                               ACT.Copy).then_inc(sp_free[K[name] % 4], 1)

            for b in range(2):
                if b:
                    halves(3)
                    put_hT(("kh",))
                    halves(5)
                else:
                    halves(8)
                c = C["w1"] + b
                sums = chunk_in(c)[0][0:NCG, 0:CMPH]
                act.activation(cmp_h[0:NCG], sums, ACT.Gelu_apprx_tanh).then_inc(pair_free[c % 2], 1)
            n_for = [15]

            def rope_stage(c):
                b = chunk_in(c)
                act.wait_ge(for_act, n_for[0])
                for t in range(NT):
                    ins = act.activation(rope_in[:, t, :], b[t][:, :], ACT.Copy)
                ins.then_inc(pair_free[c % 2], 1)
                n_for[0] += 1
            for n in range(4):
                if n == 0:
                    halves(3)
                    wait_sp(act, ("kcmp",))
                    put_hT(("vh",))
                    halves(5)
                else:
                    halves(8)
                if n == 1:
                    name = ("vcmp",)
                    wait_sp(act, name)
                    act.activation(vcmp[0:NCMP], sp_bank(name)[0:NCMP, :].rearrange("p (g d) -> p g d", g=NG), ACT.Copy)\
                       .then_inc(sp_free[K[name] % 4], 1)
                c = C["kv"] + n
                if n % 2 == 0:
                    rope_stage(c)
                    continue
                b = chunk_in(c)
                for t in range(NT):
                    ins = act.activation(vs[:, n // 2, t, :], b[t][:, :], ACT.Copy)
                ins.then_inc(pair_free[c % 2], 1)

            def from_dve():
                n_for[0] += 1
                act.wait_ge(for_act, n_for[0])

            def exps(g, t):
                kn = (t + 1) * P
                from_dve()
                for h in range(HPG):
                    ins = act.activation(sc_cmp[:, h, :], sc_cmp[:, h, :], ACT.Exp, bias=sm[:, 4, h:h + 1],
                                         accum_out=sm[:, 5, h:h + 1])
                done(ins)
                for b in range(2):
                    from_dve()
                    v = sc_buf[b][:, 0:HPG * kn].rearrange("p (h n) -> p h n", h=HPG)
                    for h in range(HPG):
                        ins = act.activation(v[:, h, :], v[:, h, :], ACT.Exp, bias=sm[:, 4, 4 + 4 * b + h:5 + 4 * b + h],
                                             accum_out=sm[:, 5, 4 + 4 * b + h:5 + 4 * b + h])
                    done(ins)

            def probs_T(g, t):
                name = ("cT", g, t)
                wait_sp(act, name)
                act.activation(pT_cmp[0:NCMP], sp_bank(name)[0:NCMP, :], ACT.Copy).then_inc(sp_free[K[name] % 4], 1)
                for b in range(2):
                    for k in range(t + 1):
                        name = ("pT", g, t, b, k)
                        wait_sp(act, name)
                        act.activation(pT_buf[b][:, k, :], sp_bank(name)[:, :], ACT.Copy).then_inc(sp_free[K[name] % 4], 1)

            def heads_out(g, t):
                put(("oT", g, t), qT[:, 4 * g:4 * g + 4, t * P:(t + 1) * P])

            halves(8)
            rope_stage(C["q"])
            for g in range(NG):
                n = 1 if g < NG - 1 else 0
                halves(n)
                if g:
                    heads_out(g - 1, 1)
                halves(2 * n)
                exps(g, 0)
                halves(n)
                probs_T(g, 0)
                halves(2 * n)
                heads_out(g, 0)
                exps(g, 1)
                halves(n)
                probs_T(g, 1)
                halves(n)
                if n:
                    rope_stage(C["q"] + g + 1)
            heads_out(NG - 1, 1)
            for t in range(NT):
                wait_sp_read(act, ("oT", NG - 1, t))
            outer("out1", KT)
            ln(2)
            split_xt(3)
            ffn(1)
            ln(3, True)

        @block.vector
        def _(dv):
            h_next = [0]
            n_own, n_pe, n_act = [0], [0], [0]

            def own(ins, i=None, per=0):
                n_own[0] += 1
                ins.then_inc(dve, 1)
                dv.wait_ge(dve, at(n_own[0], i, per))

            def to_act(ins):
                n_act[0] += 1
                ins.then_inc(for_act, 1)

            marks = [0]

            def mark():
                marks[0] += 1
                return dv.memset(sm[:, 0, marks[0] % 16:marks[0] % 16 + 1], 0.0)

            def to_pe(ins, name):
                n_pe[0] += 1
                assert FP[name] == n_pe[0]
                ins.then_inc(for_pe, 1)

            def halves(count, i=None, per=0):
                for _ in range(count):
                    h = h_next[0]
                    if h >= 2 * total_slabs:
                        return
                    src, slot = half_of(h)
                    dv.wait_ge(w_hi_ready, at(h + 1, i, per))
                    dv.tensor_tensor(w_lo[:, slot, :], src, w_hi[:, slot, :].bitcast(F32), ALU.subtract)\
                      .then_inc(w_lo_ready, 1)
                    h_next[0] += 1

            def loop_over(n, per_halves, body, per_own=0):
                o = n_own[0]
                with dv.Fori(0, n) as i:
                    body(i)
                assert n_own[0] == o + per_own
                n_own[0] += (n - 1) * per_own
                h_next[0] += (n - 1) * per_halves

            def chunk_in(c, i=None, per=0):
                dv.wait_ge(half_used, at(chunk_end[c], i, 16 * per))
                return pair(c)

            def chunk_staged(c, i=None, per=0):
                dv.wait_ge(pair_free[c % 2], at(c // 2 + 1, i, per))

            def bc(ap, n):
                return ap.unsqueeze(1).to_broadcast([ap.shape[0], n, ap.shape[-1]])

            def over(ap, n):
                return ap.unsqueeze(2).to_broadcast([ap.shape[0], ap.shape[1], n])

            def split_xt(m):
                if m:
                    dv.wait_ge(gb_in, 48 * m)
                for q in range(4):
                    if m == 0:
                        dv.wait_ge(xt_hi_ready, q + 1)
                        for u in (2 * q, 2 * q + 1):
                            v = slice(2 * u, 2 * u + 2)
                            dv.tensor_tensor(xt_lo[:, v, :], sp_bank(("xT", m, u))[:, :].rearrange("p (a t) -> p a t", a=2),
                                             xt_hi[:, v, :].bitcast(F32), ALU.subtract).then_inc(sp_free[K[("xT", m, u)] % 4], 1)
                        mark().then_inc(xt_lo_ready, 1)
                        continue
                    for u in (2 * q, 2 * q + 1):
                        name = ("xT", m, u)
                        wait_sp(dv, name)
                        for a in range(2):
                            kt = 2 * u + a
                            src = sp_bank(name)[:, a * SEQ:(a + 1) * SEQ]
                            ins = dv.tensor_scalar(yt[:, kt, :], src, lnT[:, 0, kt:kt + 1], lnT[:, 1, kt:kt + 1],
                                                   ALU.mult, ALU.add)
                        ins.then_inc(sp_free[K[name] % 4], 1)
                    if q < LEAD:
                        halves(1)
                    dv.wait_ge(xt_hi_ready, 4 * m + q + 1)
                    v = slice(4 * q, 4 * q + 4)
                    dv.tensor_tensor(xt_lo[:, v, :], yt[:, v, :], xt_hi[:, v, :].bitcast(F32), ALU.subtract)\
                      .then_inc(xt_lo_ready, 1)

            def outer(name, n):
                src = outer_src(name)

                def split(kt, i=None):
                    dv.wait_ge(a_hi_ready, at(A0[name] + kt + 1, i, 4))
                    col = kt if i is None else ds(i * 4 + kt, 1)
                    s_ = src[:, col, :]
                    dv.tensor_tensor(a_lo[:, kt % 4, :], s_, a_hi[:, kt % 4, :].bitcast(F32), ALU.subtract)\
                      .then_inc(a_lo_ready, 1)

                def quad(kt, i=None):
                    for j in range(4):
                        if kt + j + 1 < n:
                            split(kt + j + 1, i)
                        halves(2 if kt + j < n - 2 or i is not None else n - 1 - kt - j, i, 8)
                split(0)
                loop_over(n // 4 - 1, 8, lambda i: quad(0, i))
                quad(n - 4)

            def ln(n, last=False):
                name = ("out0", "fout0", "out1", "fout1")[n]
                if n:
                    dv.wait_ge(x_scaled, NT * n)
                else:
                    dv.wait_ge(x_in_sem, 16 * NT)

                def add(t):
                    for c in range(4):
                        v = x[:, t, c * CH:(c + 1) * CH]
                        ins = dv.scalar_tensor_tensor(v, v, ALPHA, bank[4 * t + c][:, :], ALU.mult, ALU.add)
                    own(ins)

                def moments(t):
                    for c in range(4):
                        ins = dv.bn_stats(stats[:, t, c, :], x[:, t, c * CH:(c + 1) * CH])
                    own(ins)
                    dv.bn_aggr(mv[:, t, :], stats[:, t, :, :].rearrange("p c s -> p (c s)")).then_inc(var_ready, 1)

                def scale(t):
                    dv.wait_ge(std_ready, NT * n + t + 1)
                    own(dv.reciprocal(rstd[:, t:t + 1], rstd[:, t:t + 1]))
                    if not last:
                        dv.scalar_tensor_tensor(nmr[:, t:t + 1], mv[:, t, 0:1], -1.0, rstd[:, t:t + 1], ALU.mult, ALU.mult)\
                          .then_inc(nmr_ready, 1)

                def result(t):
                    for c in range(2):
                        v, w = x[:, t, c * D // 2:(c + 1) * D // 2], slice(c * D // 2, (c + 1) * D // 2)
                        own(dv.scalar_tensor_tensor(v, v, mv[:, t, 0:1], gb[:, 0, w], ALU.subtract, ALU.mult))
                        dv.scalar_tensor_tensor(v, v, rstd[:, t:t + 1], gb[:, 1, w], ALU.mult, ALU.add).then_inc(out_ready, 1)

                dv.wait_ge(first_whole, n + 1)
                add(0)
                moments(0)
                dv.wait_ge(half_used, 2 * (S[name] + (FT if n % 2 else KT)))
                add(1)
                scale(0)
                moments(1)
                if last:
                    dv.wait_ge(gb_in, 48 * (n + 1))
                    result(0)
                scale(1)
                if last:
                    result(1)

            def ffn(layer):
                c0, k0 = C[f"ffn{layer}"], K[("ffn", layer, 0)]
                n_hid = layer * (FFN // CH)

                def up(c, k, first, i=None):
                    chunk_staged(c - 1, i, 2)
                    b = chunk_in(c, i, 2)
                    if not first:
                        for a in range(2):
                            dv.wait_ge(sp_ready[(k - 2 + a) % 4], at((k - 2 + a) // 4 + 1, i, 1))
                    for t in range(NT):
                        ins = dv.tensor_tensor(hid[:, t, :], b[t][:, :], sg[:, t, :], ALU.mult)
                        ins.then_inc(hid_ready if t else pair_free[c % 2], 1)
                halves(16)
                up(c0 + 1, k0, True)

                def body(i):
                    for n in range(2):
                        halves(16, i, 32)
                        up(c0 + 3 + 2 * n, k0 + 2 + 2 * n, False, i)
                loop_over(5, 32, body)
                outer(f"fout{layer}", FT)

            dv.memset(sm[:, 15, :], 0.0).then_inc(stage_free, 2)
            halves(LEAD)
            split_xt(0)
            dv.wait_ge(consts, 3)
            halves(2)
            halves(8 * 2)
            dv.wait_ge(small_in, 16 * 5)

            def conv(dst, src, w, taps, i=None, per=0, per_halves=0):
                for tap in range(taps):
                    for f in range(4):
                        wv = w(f, taps - 1 - tap)
                        if tap == 0:
                            ins = dv.tensor_scalar(dst[:, f, :], src[:, f, :], wv, None, ALU.mult)
                        else:
                            ins = dv.scalar_tensor_tensor(dst[:, f, tap:], src[:, f, 0:SEQ - tap], wv, dst[:, f, tap:],
                                                          ALU.mult, ALU.add)
                    if tap < taps - 1:
                        own(ins, i, per)
                    if tap == 1:
                        halves(1, i, per_halves)
                ins.then_inc(stage_free, 1)

            def qkv_turn(i):
                for j in range(2):
                    halves(7, i, 16)
                    chunk_staged(C["qkv"] + j, i, 1)

                    def w(f, tap):
                        return misc_w[:, ds(i * 32 + 16 * j + 4 * f + tap, 1)]
                    conv(qkvT[:, ds(i * 8 + 4 * j, 4), :], conv_in[:, j, :, :], w, DNK, i, 6, 16)
            halves(1)
            loop_over(3, 16, qkv_turn, per_own=6)
            s_, abs_, g_ = sm[:, 15, :], sm[:, 8, :], sm[:, 3, :]

            def th(ap):
                return ap.rearrange("p (t h) -> p t h", t=NT)

            def unit(u):
                name = ("norm", u)
                wait_sp_read(dv, name)
                r = norm_q.rearrange("p h d -> p (h d)")
                v = qkvT[:, 2 * u:2 * u + 2, :].rearrange("p f t -> p (f t)")
                own(dv.reciprocal(r, r))
                to_act(dv.scalar_tensor_tensor(v, r, SCALE if u < 4 else 1.0, v, ALU.mult, ALU.mult))

            def halves_and_units(m, first=5):
                halves(first)
                unit(2 * m - 2)
                halves(3)
                unit(2 * m - 1)

            for j in range(2):
                if j:
                    halves_and_units(3)
                else:
                    halves(7)
                halves_and_units(3 * j + 1)
                c = C["sc"] + 3 * j
                chunk_staged(c)
                b = chunk_in(c + 1)
                for a in range(2):
                    v = conv_in[:, j, 2 * a:2 * a + 2, :].rearrange("p f t -> p (f t)")
                    ins = dv.tensor_tensor(v, v, b[a][:, :], ALU.mult)
                ins.then_inc(pair_free[(c + 1) % 2], 1)
                dv.wait_ge(pair_free[(c + 1) % 2], (c + 1) // 2 + 1)
                conv(conv_out, conv_in[:, j, :, :], lambda f, tap: misc_w[:, 96 + 3 * (4 * j + f) + tap:97 + 3 * (4 * j + f) + tap], SCK)
                if j == 0:
                    halves_and_units(2, 4)
                else:
                    wait_sp_read(dv, ("ba",))
                    own(dv.tensor_tensor(th(s_), sm[:, 0:2, 8:16], bc(misc_w[:, 128:136], NT), ALU.add))
                    to_act(dv.scalar_tensor_tensor(abs_, s_, -1.0, s_, ALU.mult, ALU.max))
                    halves(3)
                    dv.wait_ge(from_act, 3)
                    own(dv.scalar_tensor_tensor(s_, s_, 0.0, sm[:, 9, :], ALU.max, ALU.add))
                    to_pe(dv.scalar_tensor_tensor(th(g_), th(s_), -1.0, bc(misc_w[:, 120:128], NT), ALU.mult, ALU.mult), ("g",))
                    halves(4)
                dv.wait_ge(stage_free, 9 + j)
                b = chunk_in(c + 2)
                for a in range(2):
                    v = conv_out[:, 2 * a:2 * a + 2, :].rearrange("p f t -> p (f t)")
                    ins = dv.tensor_tensor(yt[:, 4 * j + 2 * a:4 * j + 2 * a + 2, :].rearrange("p f t -> p (f t)"), v, b[a][:, :], ALU.mult)
                ins.then_inc(pair_free[(c + 2) % 2], 1)

            name = ("gc",)
            wait_sp(dv, name)
            b = sp_bank(name)
            gc_, ngc, egc, nbe, beta, kdec = sm[:, 4, :], sm[:, 5, :], sm[:, 6, :], sm[:, 7, :], sm[:, 2, :], sm[:, 14, 8:16]
            own(dv.tensor_copy(gc_, b[:, 0:16]))
            own(dv.tensor_scalar(ngc, gc_, -1.0, None, ALU.mult))
            dv.tensor_tensor(kdec, b[:, 16:24], gc_[:, 0:8], ALU.subtract).then_inc(sp_free[K[name] % 4], 1)
            dv.wait_ge(sp_free[K[name] % 4], K[name] // 4 + 1)
            to_act(dv.tensor_copy(sm[:, 15, 0:8], kdec))
            dv.wait_ge(from_act, 6)
            own(dv.scalar_tensor_tensor(nbe, egc, -1.0, beta, ALU.mult, ALU.mult))
            zf = z_tok.rearrange("p t h d -> p (t h) d")
            own(dv.tensor_tensor(zf, zf, bc(norm_w, NT * DNH), ALU.mult))
            for hh in range(2):
                wait_sp_read(dv, ("ktok", hh))
            own(dv.tensor_tensor(k_tok, k_tok, over(kdec, DH), ALU.mult))
            for t in range(NT):
                for hh in range(2):
                    wait_sp_read(dv, ("vtok", t, hh))
            n_from = [6]

            def sp_out(ins, name):
                ins.then_inc(sp_free[K[name] % 4], 1)

            def sp4(name):
                return sp_bank(name)[:, :].rearrange("p (h d) -> p h d", h=4)
            def heads_of(t, hh):
                return slice(8 * t + 4 * hh, 8 * t + 4 * hh + 4)
            for t, hh in units:
                _, _, _, T, _, G = tiles_of(t, hh)
                dv.tensor_tensor(G, bc(upper[:, :], 4), over(g_[:, heads_of(t, hh)], P), ALU.mult)
                to_pe(dv.tensor_tensor(T, bc(ident[:, :], 4), over(beta[:, heads_of(t, hh)], P), ALU.mult), ("rows", t, hh))
            for t, hh in units:
                Dt, AT, E, T, X, G = tiles_of(t, hh)
                name = ("row", t, hh)
                wait_sp(dv, name)
                for h in range(4):
                    n = 8 * t + 4 * hh + h
                    ins = dv.scalar_tensor_tensor(Dt[:, h, :], sp4(name)[:, h, :], ngc[:, n:n + 1], neg_lower[:, :], ALU.add, ALU.add)
                sp_out(ins, name)
                n_from[0] += 1
                dv.wait_ge(from_act, n_from[0])
                wait_sp(dv, ("kk", t, hh))
                sp_out(dv.tensor_tensor(AT, sp4(("kk", t, hh)), Dt, ALU.mult), ("kk", t, hh))
                wait_sp_read(dv, ("kk", t, hh))
                wait_sp(dv, ("beta", t, hh))
                sp_out(dv.tensor_tensor(AT, AT, sp4(("beta", t, hh)), ALU.mult), ("beta", t, hh))
                wait_sp(dv, ("kq", t, hh))
                sp_out(dv.tensor_tensor(Dt, Dt, sp4(("kq", t, hh)), ALU.mult), ("kq", t, hh))
                wait_sp_read(dv, ("beta", t, hh))
                own(dv.tensor_tensor(E, AT, bc(blk_mask[:, 0, :], 4), ALU.mult))
                to_pe(dv.tensor_tensor(X, bc(ident[:, :], 4), E, ALU.subtract), ("m", t, 0, hh))
            for t, hh in units:
                Dt, AT, E, T, X, G = tiles_of(t, hh)
                name = ("eT", t, hh)
                wait_sp(dv, name)
                sp_out(dv.tensor_tensor(T, bc(ident[:, :], 4), sp4(name), ALU.subtract), name)
                to_pe(dv.tensor_tensor(E, AT, bc(blk_mask[:, 1, :], 4), ALU.mult), ("m", t, 1, hh))
            for n in range(1, len(BLOCKS)):
                for t, hh in units:
                    Dt, AT, E, T, X, G = tiles_of(t, hh)
                    wait_sp(dv, ("x", t, n, hh))
                    if n < len(BLOCKS) - 1:
                        wait_sp(dv, ("t", t, n, hh))
                        sp_out(dv.tensor_tensor(X, X, sp4(("x", t, n, hh)), ALU.subtract), ("x", t, n, hh))
                        sp_out(dv.tensor_tensor(T, T, sp4(("t", t, n, hh)), ALU.subtract), ("t", t, n, hh))
                        to_pe(dv.tensor_tensor(E, AT, bc(blk_mask[:, n + 1, :], 4), ALU.mult), ("m", t, n + 1, hh))
                    else:
                        sp_out(dv.tensor_tensor(X, X, sp4(("x", t, n, hh)), ALU.subtract), ("x", t, n, hh))
            for t in range(NT):
                heads = [heads_of(t, hh) for hh in range(2)]
                tiles = [tiles_of(t, hh) for hh in range(2)]
                for hh in range(2):
                    Dt, AT, E, T, X, G = tiles[hh]
                    ins = dv.tensor_tensor(T, v_tok[:, t, 4 * hh:4 * hh + 4, :], over(beta[:, heads[hh]], DH), ALU.mult)
                    if t == 0:
                        to_pe(ins, ("rhs", t, hh))
                        continue
                    own(ins)
                    wait_sp(dv, ("ks", hh))
                    for h in range(4):
                        n = 8 * t + 4 * hh + h
                        ins = dv.scalar_tensor_tensor(T[:, h, :], sp4(("ks", hh))[:, h, :], nbe[:, n:n + 1], T[:, h, :], ALU.mult, ALU.add)
                    sp_out(ins, ("ks", hh))
                    wait_sp(dv, ("qs", hh))
                    sp_out(dv.tensor_tensor(AT, sp4(("qs", hh)), over(egc[:, heads[hh]], DH), ALU.mult), ("qs", hh))
                    wait_sp_read(dv, ("ks", hh))
                    wait_sp_read(dv, ("qs", hh))
                    to_pe(mark(), ("rhs", t, hh))
                for hh in range(2):
                    Dt, AT, E, T, X, G = tiles[hh]
                    name = ("o", t, hh)
                    wait_sp(dv, name)
                    if t:
                        sp_out(dv.tensor_tensor(AT, AT, sp4(name), ALU.add), name)
                    else:
                        sp_out(dv.tensor_copy(AT, sp4(name)), name)
                        wait_sp(dv, ("s", hh))
                        sp_out(dv.tensor_copy(state[:, 4 * hh:4 * hh + 4, :], sp4(("s", hh))), ("s", hh))
                    wait_sp_read(dv, name)
                    own(dv.tensor_tensor(E, AT, AT, ALU.mult))
                    to_act(dv.tensor_reduce(sm[:, 10, 4 * hh:4 * hh + 4], E, AX.X, ALU.add))
                for hh in range(2):
                    Dt, AT, E, T, X, G = tiles[hh]
                    n_from[0] += 1
                    dv.wait_ge(from_act, n_from[0])
                    r = sm[:, 11, 4 * hh:4 * hh + 4]
                    own(dv.reciprocal(r, r))
                    for h in range(4):
                        ins = dv.scalar_tensor_tensor(AT[:, h, :], AT[:, h, :], r[:, h:h + 1], z_tok[:, t, 4 * hh + h, :], ALU.mult, ALU.mult)
                    to_pe(ins, ("on", t, hh))
            for hh in range(2):
                wait_sp(dv, ("y", 1, hh))
            mark().then_inc(gb_free, 1)
            outer("out0", KT)
            ln(0)
            split_xt(1)
            mark().then_inc(gb_free, 1)
            ffn(0)
            ln(1, stop == "l0")
            if stop == "l0":
                return

            split_xt(2)
            halves(3)
            dv.wait_ge(nsa_in, 16 * 6)
            rows = [(slice(0, P), slice(0, 2)), (slice(0, NCG), slice(2, 3))]
            for r, n in rows:
                for a in range(n.start, n.stop):
                    own(dv.tensor_copy(sm[r, 15, a:a + 1], misc_w[r, 64 + a:65 + a].bitcast(I32)))
                    own(dv.tensor_scalar(angle[r, a, :], misc_w[r, 0:64], sm[r, 15, a:a + 1], None, ALU.mult))
                av, tv = angle[r, n, :], turns[r, n, :]
                own(dv.tensor_scalar(tv, av, float(1 / (2 * np.pi)), ROUND, ALU.mult, ALU.add))
                own(dv.tensor_scalar(tv, tv, ROUND, None, ALU.subtract))
                for part_ in (TWO_PI_1, TWO_PI_2, TWO_PI_3):
                    own(dv.scalar_tensor_tensor(av, tv, -part_, av, ALU.mult, ALU.add))
                own(dv.tensor_scalar(av, av, PI, -PI, ALU.min, ALU.max))
                ins = dv.scalar_tensor_tensor(tv, av, -1.0, av, ALU.mult, ALU.max)
                if n.start == 0:
                    own(ins)
            to_act(ins)
            halves(5)
            def block_sum(b):
                chunk_staged(C["vc" if b else "kc"])
                for hf in range(2):
                    lo = slice(16 * hf, 16 * hf + 16)
                    for g in range(NG):
                        src = kcT[:, b, g, 16 * hf:16 * hf + 16 * NCMP].rearrange("p (n l) -> p l n", l=16)
                        ins = dv.tensor_tensor(blk_sum[:, lo, g * NCMP:(g + 1) * NCMP], src, over(posT[:, b, lo], NCMP), ALU.add)
                own(ins)

            def block_hi(b):
                own(dv.tensor_copy(blk_hi[b][:, 0:blk_n], yt_flat[:, 0:blk_n]))

            def block_lo(b):
                dv.tensor_tensor(blk_lo[b][:, 0:blk_n], yt_flat[:, 0:blk_n], blk_hi[b][:, 0:blk_n].bitcast(F32), ALU.subtract)\
                  .then_inc(for_pe, 1)

            dv.wait_ge(x_scaled, 2 * NT)
            for b in range(2):
                for v in (blk_hi[b], blk_lo[b]):
                    dv.tensor_scalar(v[:, blk_n:blk_w], ones[:, 0:blk_w - blk_n], 0.0, None, ALU.mult)
            block_sum(0)
            block_hi(0)
            block_lo(0)
            halves(2 + 8)
            dv.wait_ge(from_act, 16)
            n_from[0] = 16
            hd = DH // 2
            for cv, sv in ((cosb, sinb), (cosc[0:NCG].unsqueeze(1), sinc[0:NCG].unsqueeze(1))):
                own(dv.tensor_copy(cv[:, :, 0:hd], cv[:, :, hd:]))
                own(dv.tensor_scalar(sv[:, :, 0:hd], sv[:, :, hd:], -1.0, None, ALU.mult))
            block_sum(1)
            halves(2)
            block_hi(1)
            halves(2)
            block_lo(1)
            halves(4)
            halves(8)
            name = ("kcmp",)
            wait_sp(dv, name)
            kb = sp_bank(name)
            rows_ = slice(0, NCG)
            ra, rb = rope_a[rows_, 0, 0:DH], rope_b[rows_, 0, 0:DH]
            dv.tensor_tensor(ra, kb[rows_, 0:DH], cosc[rows_], ALU.mult)
            dv.tensor_tensor(rb[:, 0:hd], kb[rows_, hd:DH], sinc[rows_, 0:hd], ALU.mult)
            sp_out(dv.tensor_tensor(rb[:, hd:DH], kb[rows_, 0:hd], sinc[rows_, hd:DH], ALU.mult), name)
            wait_sp_read(dv, name)
            dv.tensor_tensor(ra, ra, rb, ALU.add).then_inc(for_pe, 1)

            def rope(c):
                chunk_staged(c)
                for t in range(NT):
                    v = rope_in[:, t, :].rearrange("p (h d) -> p h d", h=4)
                    va = rope_a[:, t, :].rearrange("p (h d) -> p h d", h=4)
                    vb = rope_b[:, t, :].rearrange("p (h d) -> p h d", h=4)
                    dv.tensor_tensor(va, v, bc(cosb[:, t, :], 4), ALU.mult)
                    dv.tensor_tensor(vb[:, :, 0:hd], v[:, :, hd:DH], bc(sinb[:, t, 0:hd], 4), ALU.mult)
                    ins = dv.tensor_tensor(vb[:, :, hd:DH], v[:, :, 0:hd], bc(sinb[:, t, hd:DH], 4), ALU.mult)
                to_act(ins)
                dv.wait_ge(for_act, n_act[0])
                dv.tensor_tensor(rope_a, rope_a, rope_b, ALU.add).then_inc(for_pe, 1)

            def put_T(k, dst):
                for a in range(2):
                    dv.wait_ge(sp_ready[(k + a) % 4], (k + a) // 4 + 1)
                    dv.tensor_copy(dst(a), bank[4 + (k + a) % 4][:, :].rearrange("p (h t) -> p h t", h=2)).then_inc(sp_free[(k + a) % 4], 1)
            for b in range(2):
                halves(8)
                if b == 0:
                    name = ("kcmpT",)
                    wait_sp(dv, name)
                    sp_out(dv.tensor_copy(kcmpT[:, 0:NCG], sp_bank(name)[:, 0:NCG]), name)
                rope(C["kv"] + 2 * b)
                halves(8)
                put_T(K[("kv", b, 0)], lambda a: ksT[:, b, 2 * a:2 * a + 2, :])

            wait_sp_read(dv, ("gates",))
            nmax, sums, cf = sm[:, 4, :], sm[:, 5, :], sm[:, 6, :]
            gate_v = gates.rearrange("p t (h b) -> p t h b", b=3)
            def before(g, t):
                return (g, 0) if t else (g - 1, 1)

            def scores(g, t):
                kn = (t + 1) * P
                if g or t:
                    wait_sp(dv, ("co", *before(g, t)))
                name = ("c", g, t)
                wait_sp(dv, name)
                v = sp_bank(name)[:, 0:HPG * NCMP].rearrange("p (h n) -> p h n", h=HPG)
                sp_out(dv.scalar_tensor_tensor(sc_cmp, v, SCALE, bc(neg_cmp[:, t, :], HPG), ALU.mult, ALU.add), name)
                wait_sp_read(dv, name)
                to_act(dv.tensor_reduce(nmax[:, 0:4], sc_cmp, AX.X, ALU.max, negate=True))
                for b in range(2):
                    v = sc_buf[b][:, 0:HPG * kn].rearrange("p (h n) -> p h n", h=HPG)
                    hp = HPG // (t + 1)
                    for k in range(t + 1):
                        name = ("s", g, t, b, k)
                        wait_sp(dv, name)
                        mask = neg_upper.rearrange("p a n -> p (a n)")[:, SEQ - kn:SEQ]
                        sp_out(dv.scalar_tensor_tensor(v[:, hp * k:hp * k + hp, :], sp_bank(name)[:, :].rearrange("p (h n) -> p h n", h=hp),
                                                       SCALE, bc(mask, hp), ALU.mult, ALU.add), name)
                    for k in range(t + 1):
                        wait_sp_read(dv, ("s", g, t, b, k))
                    to_act(dv.tensor_reduce(nmax[:, 4 + 4 * b:8 + 4 * b], v, AX.X, ALU.max, negate=True))

            def masked(g, t):
                n_from[0] += 1
                dv.wait_ge(from_act, n_from[0])
                dv.tensor_tensor(sc_cmp, sc_cmp, bc(ok_cmp[:, t, :], HPG), ALU.mult).then_inc(for_pe, 1)

            def weights(g, t):
                n_from[0] += 2
                dv.wait_ge(from_act, n_from[0])
                own(dv.reciprocal(cf[:, 0:12], sums[:, 0:12]))
                own(dv.tensor_tensor(cf[:, 0:12].rearrange("p (b h) -> p b h", b=3), cf[:, 0:12].rearrange("p (b h) -> p b h", b=3),
                                     gate_v[:, t, 4 * g:4 * g + 4, :].rearrange("p h b -> p b h"), ALU.mult))

            def branches(g, t):
                if g or t:
                    wait_sp(dv, ("oT", *before(g, t)))
                for b, name in enumerate((("co", g, t), ("po", g, t, 0), ("po", g, t, 1))):
                    wait_sp(dv, name)
                    for h in range(HPG):
                        w = cf[:, 4 * b + h:4 * b + h + 1]
                        if b == 0:
                            ins = dv.tensor_scalar(o_buf[:, h, :], sp4(name)[:, h, :], w, None, ALU.mult)
                        else:
                            ins = dv.scalar_tensor_tensor(o_buf[:, h, :], sp4(name)[:, h, :], w, o_buf[:, h, :], ALU.mult, ALU.add)
                    sp_out(ins, name)
                    wait_sp_read(dv, name)
                mark().then_inc(for_pe, 1)

            halves(8)
            rope(C["q"])
            for g in range(NG):
                n = 1 if g < NG - 1 else 0
                halves(n)
                put_T(K[("q", 2 * g)], lambda a: qT[:, 4 * g + 2 * a:4 * g + 2 * a + 2, :])
                halves(2 * n)
                scores(g, 0)
                masked(g, 0)
                halves(n)
                weights(g, 0)
                halves(n)
                branches(g, 0)
                halves(n)
                scores(g, 1)
                masked(g, 1)
                halves(n)
                weights(g, 1)
                halves(n)
                branches(g, 1)
                if n:
                    rope(C["q"] + g + 1)
            mark().then_inc(gb_free, 1)
            outer("out1", KT)
            ln(2)
            split_xt(3)
            mark().then_inc(gb_free, 1)
            ffn(1)
            ln(3, True)

        @block.tensor
        def _(pe):
            n_pe = [0]

            def sp_use(name, i=None, per=0):
                k = K[name]
                if k >= 4:
                    pe.wait_ge(sp_free[k % 4], at(k // 4, i, per // 4))
                return bank[4 + k % 4]

            def sp_done(ins, name):
                ins.then_inc(sp_ready[K[name] % 4], 1)

            def handed(name):
                pe.wait_ge(for_pe, FP[name])

            def used(ins, h=None):
                ins.then_inc(half_used, 1)

            def passes(dst, l_hi, l_lo, r_hi, r_lo, start, stop, shared=False):
                pe.matmul(dst, l_hi, r_hi, start=start, stop=False, skip_group_check=shared)
                pe.matmul(dst, l_hi, r_lo, start=False, stop=False, skip_group_check=shared)
                return pe.matmul(dst, l_lo, r_hi, start=False, stop=stop, skip_group_check=shared)

            def xT(m):
                if m == 0:
                    pe.wait_ge(ident_ready, 1)
                    pe.wait_ge(x_in_sem, 16 * NT)
                for u in range(8):
                    if m and u % 2 == 0:
                        pe.wait_ge(x_normed, 5 * (m - 1) + 2 + u // 2)
                    name = ("xT", m, u)
                    b = sp_use(name)
                    for a in range(2):
                        for t in range(NT):
                            ins = pe.transpose(b[:, a * SEQ + t * P:a * SEQ + (t + 1) * P],
                                               x[:, t, (2 * u + a) * P:(2 * u + a + 1) * P], ident[:, :])
                    sp_done(ins, name)

            def slab_in_chunk(s, quad, b, by_token, i, per, m, after):
                if m is not None:
                    pe.wait_ge(xt_lo_ready, 4 * m + quad + 1)
                for hf in range(2):
                    h = 2 * (s + quad) + hf
                    pe.wait_ge(w_lo_ready, at(h + 1, i, 2 * per))
                    for kk in range(2):
                        kt = 4 * quad + 2 * hf + kk
                        cols = slice(kk * CH, (kk + 1) * CH)
                        hi, lo = w_hi[:, h % HL_SLOTS, cols], w_lo[:, h % HL_SLOTS, cols]
                        if by_token:
                            for t in range(NT):
                                v = slice(t * P, (t + 1) * P)
                                ins = passes(b[t][:, :], xt_hi[:, kt, v], xt_lo[:, kt, v], hi, lo, kt == 0, kt == KT - 1)
                        else:
                            for f in range(4):
                                v = slice(f * P, (f + 1) * P)
                                ins = passes(b[f // 2][:, f % 2 * SEQ:(f % 2 + 1) * SEQ], hi[:, v], lo[:, v],
                                             xt_hi[:, kt, :], xt_lo[:, kt, :], kt == 0 and f % 2 == 0, kt == KT - 1, True)
                    used(ins)
                    if 2 * quad + hf + 1 in (after or {}):
                        after[2 * quad + hf + 1]()

            def chunk(s, c, by_token, i=None, per=0, between=None, m=None, after=None):
                if c >= 2:
                    pe.wait_ge(pair_free[c % 2], at(c // 2, i, per // 2))
                b = pair(c)
                if between:
                    after = {2: between}
                for quad in range(4):
                    slab_in_chunk(s, quad, b, by_token, i, 4 * per, m, after)

            def small(s, c):
                if c >= 2:
                    pe.wait_ge(pair_free[c % 2], c // 2)
                b = pair(c)[0]
                for hf in range(2):
                    h = 2 * s + hf
                    pe.wait_ge(w_lo_ready, h + 1)
                    for kk in range(KT // 2):
                        kt = hf * (KT // 2) + kk
                        cols = slice(kk * P, (kk + 1) * P)
                        ins = passes(b[:, 0:SEQ], w_hi[:, h % HL_SLOTS, cols], w_lo[:, h % HL_SLOTS, cols],
                                     xt_hi[:, kt, :], xt_lo[:, kt, :], kt == 0, kt == KT - 1)
                    used(ins)

            def small_T(name, c, src):
                pe.wait_ge(pair_free[c % 2], c // 2 + 1)
                b = sp_use((name,))
                for t in range(NT):
                    ins = pe.transpose(b[:, t * P:(t + 1) * P], src[:, t * P:(t + 1) * P], ident[:, :])
                sp_done(ins, (name,))

            def outer(name, n, layer):
                for b in range(4):
                    last = max(k for k in ks_before[name] if k % 4 == b)
                    pe.wait_ge(sp_free[b], last // 4 + 1)
                c = chunks_before[name]
                for p in range(2):
                    pe.wait_ge(pair_free[p], (c - p + 1) // 2)

                def tile(kt, tokens, i=None):
                    pe.wait_ge(a_lo_ready, at(A0[name] + kt + 1, i, 4))
                    for hf in range(2):
                        h = 2 * (S[name] + kt) + hf
                        pe.wait_ge(w_lo_ready, at(h + 1, i, 8))
                        for cc in range(2):
                            cols = slice(cc * CH, (cc + 1) * CH)
                            for t in tokens:
                                v = slice(t * P, (t + 1) * P)
                                ins = passes(bank[4 * t + 2 * hf + cc][:, :], a_hi[:, kt % 4, v], a_lo[:, kt % 4, v],
                                             w_hi[:, h % HL_SLOTS, cols], w_lo[:, h % HL_SLOTS, cols],
                                             i is None and kt == 0, i is None and kt == n - 1)
                        if tokens[-1] == NT - 1:
                            used(ins)
                    return ins

                for kt in range(4):
                    tile(kt, range(NT))
                with pe.Fori(0, n // 4 - 2) as i:
                    for kt in range(4, 8):
                        tile(kt, range(NT), i)
                for kt in range(n - 4, n - 2):
                    tile(kt, range(NT))
                for t in range(NT):
                    for kt in range(n - 2, n):
                        ins = tile(kt, range(t, t + 1))
                        if t == 0 and kt == n - 1:
                            ins.then_inc(first_whole, 1)

            def ffn(layer):
                s0, c0 = S[f"ffn{layer}"], C[f"ffn{layer}"]
                n_hid = layer * (FFN // CH)

                def hidden_T(pair_no, n_h, i=None):
                    pe.wait_ge(hid_ready, at(n_h, i, 2))
                    for a in range(2):
                        name = ("ffn", layer, 2 * pair_no + a)
                        b = sp_use(name, i, 4)
                        for f in range(2):
                            for t in range(NT):
                                ins = pe.transpose(b[:, f * SEQ + t * P:f * SEQ + (t + 1) * P],
                                                   hid[:, t, (2 * a + f) * P:(2 * a + f + 1) * P], ident[:, :])
                        sp_done(ins, name)
                for n in range(2):
                    chunk(s0 + 4 * n, c0 + n, True, m=None if n else 2 * layer + 1)
                with pe.Fori(0, 5) as i:
                    for n in range(2):
                        chunk(s0 + 8 + 8 * n, c0 + 2 + 2 * n, True, i, 4, lambda: hidden_T(n, n_hid + n + 1, i))
                        chunk(s0 + 12 + 8 * n, c0 + 3 + 2 * n, True, i, 4)
                hidden_T(10, n_hid + 11)
                outer(f"fout{layer}", FT, layer)

            order = {"out0": ("y", 1, 1), "fout0": ("ffn", 0, 21), "out1": ("oT", NG - 1, NT - 1), "fout1": ("ffn", 1, 21)}
            ks_before = {n: range(K[last] + 1) for n, last in order.items()}
            chunks_before = {"out0": C["ffn0"], "fout0": C["kc"], "out1": C["ffn1"], "fout1": C["fout1"]}

            xT(0)
            chunk(S["z0"], C["z0"], True, m=0)
            small(S["ba"], C["ba"])
            chunk(S["z1"], C["z1"], True, between=lambda: small_T("ba", C["ba"], ba_out))
            with pe.Fori(0, 3) as i:
                for j in range(2):
                    chunk(S["qkv"] + 4 * j, C["qkv"] + j, False, i, 2)

            def squares_sum(u):
                pe.wait_ge(act_done, u + 1)
                name = ("norm", u)
                b = sp_use(name)
                sp_done(pe.matmul(b[:, :], ones[:, :], norm_sq.rearrange("p h d -> p (h d)"), start=True, stop=True), name)

            def decays():
                handed(("g",))
                b = sp_use(("gc",))
                pe.matmul(b[:, 0:16], upper[:, :], sm[:, 3, :], start=True, stop=True)
                sp_done(pe.matmul(b[:, 16:24], ones[:, :], sm[:, 3, 0:8], start=True, stop=True), ("gc",))

            for n in range(6):
                if n == 0:
                    after = None
                elif n < 5:
                    after = {3: lambda: squares_sum(2 * n - 2), 6: lambda: squares_sum(2 * n - 1)}
                else:
                    after = {5: decays}
                chunk(S["sc"] + 4 * n, C["sc"] + n, False, after=after)

            pe.wait_ge(for_act, 8)
            pe.wait_ge(silu_done, 6)

            def transposes(name, srcs, rows=P):
                b = sp_use(name)
                for h, src in enumerate(srcs):
                    ins = pe.transpose(b[0:rows, h * P:(h + 1) * P], src, ident[:, :])
                sp_done(ins, name)
            for hh in range(2):
                transposes(("ktok", hh), [qkvT[:, 8 + 4 * hh + h, 0:P] for h in range(4)])
            for t in range(NT):
                for hh in range(2):
                    transposes(("vtok", t, hh), [vT[:, 4 * hh + h, t * P:(t + 1) * P] for h in range(4)])

            def by_head(name, lhs, rhs):
                b = sp_use(name)
                for h in range(4):
                    ins = pe.matmul(b[:, h * P:(h + 1) * P], lhs(h), rhs(h), start=True, stop=True)
                sp_done(ins, name)

            def flat(tile):
                return tile.rearrange("p h d -> p (h d)")
            for t, hh in units:
                v = slice(t * P, (t + 1) * P)
                _, _, _, T, _, G = tiles_of(t, hh)
                handed(("rows", t, hh))
                for name, m in (("row", G), ("beta", T)):
                    b = sp_use((name, t, hh))
                    sp_done(pe.matmul(b[:, :], ones[:, :], flat(m), start=True, stop=True), (name, t, hh))
                by_head(("kk", t, hh), lambda h: qkvT[:, 8 + 4 * hh + h, v], lambda h: qkvT[:, 8 + 4 * hh + h, v])
                by_head(("kq", t, hh), lambda h: qkvT[:, 8 + 4 * hh + h, v], lambda h: qkvT[:, 4 * hh + h, v])
            for t, hh in units:
                handed(("m", t, 0, hh))
                transposes(("eT", t, hh), [tiles_of(t, hh)[2][:, h, :] for h in range(4)])
            for n in range(1, len(BLOCKS)):
                for t, hh in units:
                    _, _, E, T, X, G = tiles_of(t, hh)
                    handed(("m", t, n, hh))
                    by_head(("g", t, n, hh), lambda h: E[:, h, :], lambda h: T[:, h, :])
                for t, hh in units:
                    _, _, E, T, X, G = tiles_of(t, hh)
                    wait_sp_read(pe, ("g", t, n, hh))
                    by_head(("x", t, n, hh), lambda h: G[:, h, :], lambda h: X[:, h, :])
                    if n < len(BLOCKS) - 1:
                        by_head(("t", t, n, hh), lambda h: X[:, h, :], lambda h: G[:, h, :])
            for t in range(NT):
                v = slice(t * P, (t + 1) * P)
                tiles = [tiles_of(t, hh) for hh in range(2)]
                if t:
                    for hh in range(2):
                        wait_sp_read(pe, ("s", hh))
                        by_head(("ks", hh), lambda h: qkvT[:, 8 + 4 * hh + h, v], lambda h: state[:, 4 * hh + h, :])
                        by_head(("qs", hh), lambda h: qkvT[:, 4 * hh + h, v], lambda h: state[:, 4 * hh + h, :])
                for hh in range(2):
                    _, _, E, T, X, G = tiles[hh]
                    handed(("rhs", t, hh))
                    by_head(("v", t, hh), lambda h: X[:, h, :], lambda h: T[:, h, :])
                for hh in range(2):
                    Dt, G = tiles[hh][0], tiles[hh][5]
                    wait_sp_read(pe, ("v", t, hh))
                    by_head(("o", t, hh), lambda h: Dt[:, h, :], lambda h: G[:, h, :])
                    if t == 0:
                        by_head(("s", hh), lambda h: k_tok[:, 4 * hh + h, :], lambda h: G[:, h, :])
                for hh in range(2):
                    handed(("on", t, hh))
                    transposes(("y", t, hh), [tiles[hh][1][:, h, :] for h in range(4)])
            outer("out0", KT, 0)
            xT(1)
            ffn(0)
            if stop == "l0":
                return

            xT(2)
            chunk(S["kc"], C["kc"], False, m=2)
            small(S["gates"], C["gates"])
            chunk(S["vc"], C["vc"], False, between=lambda: small_T("gates", C["gates"], gates_out))
            n_fpe = n_fp

            def hidden_T(name, c):
                pe.wait_ge(pair_free[c % 2], c // 2 + 1)
                b = sp_use(name)
                for k in range(2):
                    ins = pe.transpose(b[:, 64 * k:64 * k + NCG], cmp_h[0:NCG, k * P:(k + 1) * P], ident[0:NCG, 0:NCG])
                sp_done(ins, name)

            def keys_cmp():
                name = ("kcmp",)
                pe.wait_ge(w2_in, 16 * 2)
                wait_sp_read(pe, ("kh",))
                b = sp_use(name)
                for k in range(2):
                    ins = pe.matmul(b[0:NCG, 0:DH], cmp_hT[:, k, 0:NCG], w2[:, 0, k, :], start=k == 0, stop=k == 1)
                sp_done(ins, name)

            def keys_cmp_T():
                nonlocal n_fpe
                n_fpe += 1
                pe.wait_ge(for_pe, n_fpe)
                name = ("kcmpT",)
                b = sp_use(name)
                sp_done(pe.transpose(b[:, 0:NCG], rope_a[0:NCG, 0, 0:DH], ident[0:NCG, 0:NCG]), name)

            def values_cmp():
                name = ("vcmp",)
                wait_sp_read(pe, ("vh",))
                b = sp_use(name)
                for g in range(NG):
                    for k in range(2):
                        ins = pe.matmul(b[0:NCMP, g * DH:(g + 1) * DH], cmp_hT[:, k, g * NCMP:(g + 1) * NCMP],
                                        w2[:, 1, k, :], start=k == 0, stop=k == 1)
                sp_done(ins, name)

            for b_ in range(2):
                c = C["w1"] + b_
                pe.wait_ge(pair_free[c % 2], c // 2)
                b = pair(c)[0]
                n_fpe += 1
                pe.wait_ge(for_pe, n_fpe)
                for q in range(8):
                    h = 2 * (S["w1"] + 4 * b_) + q
                    pe.wait_ge(w_lo_ready, h + 1)
                    for ll in range(4):
                        l = 4 * q + ll
                        cols, v = slice(ll * CMPH, (ll + 1) * CMPH), slice(l * NCG, l * NCG + P)
                        ins = passes(b[:, 0:CMPH], blk_hi[b_][:, v], blk_lo[b_][:, v], w_hi[:, h % HL_SLOTS, cols],
                                     w_lo[:, h % HL_SLOTS, cols], l == 0, l == CMPB - 1)
                    used(ins)
                    if b_ == 1 and q == 2:
                        hidden_T(("kh",), C["w1"])
                    if b_ == 1 and q == 5:
                        keys_cmp()

            def heads_T(names):
                for a, name in enumerate(names):
                    b = sp_use(name)
                    for h in range(2):
                        for t in range(NT):
                            ins = pe.transpose(b[:, h * SEQ + t * P:h * SEQ + (t + 1) * P],
                                               rope_a[:, t, (2 * a + h) * P:(2 * a + h + 1) * P], ident[:, :])
                    sp_done(ins, name)

            def turned(names):
                nonlocal n_fpe
                n_fpe += 1
                pe.wait_ge(for_pe, n_fpe)
                heads_T(names)
            def first():
                keys_cmp_T()
                hidden_T(("vh",), C["w1"] + 1)

            def second():
                if b_ == 0:
                    values_cmp()
                turned([("kv", b_, a) for a in range(2)])
            for b_ in range(2):
                chunk(S["kv"] + 8 * b_, C["kv"] + 2 * b_, True, between=None if b_ else first)
                chunk(S["kv"] + 8 * b_ + 4, C["kv"] + 2 * b_ + 1, True, between=second)
            chunk(S["q"], C["q"], True)
            n_fa = 16

            def scores(g, t):
                v = slice(t * P, (t + 1) * P)
                if t == 0:
                    for a in range(2):
                        wait_sp_read(pe, ("q", 2 * g + a))
                name = ("c", g, t)
                b = sp_use(name)
                for h in range(HPG):
                    ins = pe.matmul(b[:, h * NCMP:(h + 1) * NCMP], qT[:, 4 * g + h, v], kcmpT[:, g * NCMP:(g + 1) * NCMP], start=True, stop=True)
                sp_done(ins, name)
                kn = (t + 1) * P
                hp = HPG // (t + 1)
                for br in range(2):
                    for k in range(t + 1):
                        name = ("s", g, t, br, k)
                        b = sp_use(name)
                        for h in range(hp):
                            ins = pe.matmul(b[:, h * kn:(h + 1) * kn], qT[:, 4 * g + hp * k + h, v], ksT[:, br, g, 0:kn], start=True, stop=True)
                        sp_done(ins, name)

            def probs_T(g, t):
                nonlocal n_fpe, n_fa
                kn = (t + 1) * P
                n_fpe += 1
                pe.wait_ge(for_pe, n_fpe)
                transposes(("cT", g, t), [sc_cmp[:, h, :] for h in range(HPG)], NCMP)
                for br in range(2):
                    pe.wait_ge(from_act, n_fa + 2 + br)
                    for k in range(t + 1):
                        p_ = sc_buf[br][:, 0:HPG * kn].rearrange("p (h n) -> p h n", h=HPG)
                        transposes(("pT", g, t, br, k), [p_[:, h, k * P:(k + 1) * P] for h in range(HPG)])
                n_fa += 3

            def outputs(g, t):
                name = ("co", g, t)
                wait_sp_read(pe, ("cT", g, t))
                b = sp_use(name)
                for h in range(HPG):
                    ins = pe.matmul(b[:, h * P:(h + 1) * P], pT_cmp[0:NCMP, h * P:(h + 1) * P], vcmp[0:NCMP, g, :], start=True, stop=True)
                sp_done(ins, name)
                for br in range(2):
                    name = ("po", g, t, br)
                    for k in range(t + 1):
                        wait_sp_read(pe, ("pT", g, t, br, k))
                    b = sp_use(name)
                    for h in range(HPG):
                        for k in range(t + 1):
                            ins = pe.matmul(b[:, h * P:(h + 1) * P], pT_buf[br][:, k, h * P:(h + 1) * P],
                                            vs[:, br, k, g * DH:(g + 1) * DH], start=k == 0, stop=k == t)
                    sp_done(ins, name)

            def heads_out(g, t):
                nonlocal n_fpe
                n_fpe += 1
                pe.wait_ge(for_pe, n_fpe)
                transposes(("oT", g, t), [o_buf[:, h, :] for h in range(HPG)])

            for g in range(NG):
                def queries():
                    if g:
                        heads_out(g - 1, 1)
                    turned([("q", 2 * g + a) for a in range(2)])

                def next_tile():
                    heads_out(g, 0)
                    scores(g, 1)
                stages = {1: queries, 3: lambda: scores(g, 0), 4: lambda: probs_T(g, 0), 5: lambda: outputs(g, 0),
                          6: next_tile, 7: lambda: probs_T(g, 1), 8: lambda: outputs(g, 1)}
                if g < NG - 1:
                    chunk(S["q"] + 4 * (g + 1), C["q"] + g + 1, True, after=stages)
                else:
                    for stage in stages.values():
                        stage()
            heads_out(NG - 1, 1)
            outer("out1", KT, 1)
            xT(3)
            ffn(1)


_INS = ['x', 'positions', 'ln_mix_g', 'ln_mix_b', 'ln_ffn_g', 'ln_ffn_b', 'ffn_w_in', 'ffn_w_out',
        'hy_w_in', 'sc_conv_w', 'dn_conv_w', 'dn_a_log', 'dn_dt_bias', 'dn_norm_w', 'hy_w_out',
        'nsa_w_in', 'cmp_pos_k', 'cmp_w1_k', 'cmp_w2_k', 'cmp_pos_v', 'cmp_w1_v', 'cmp_w2_v', 'nsa_w_out']


def kernel(**inputs):
    import concourse.bacc as bacc
    from concourse.bass_utils import run_bass_kernel_spmd as run

    nc = bacc.Bacc("TRN2", target_bir_lowering=False, num_devices=1)
    arrays, args = {}, []

    def give(name, a):
        a = np.ascontiguousarray(a)
        arrays[name] = a
        args.append(nc.dram_tensor(name, a.shape, mybir.dt.from_np(a.dtype), kind="ExternalInput").ap())

    def by_feature(a):
        a = np.asarray(a)
        return a.reshape(a.shape[0], -1, P).transpose(2, 1, 0)

    laid = dict(inputs)
    for name in ("sc_conv_w", "dn_conv_w"):
        laid[name] = by_feature(inputs[name][0]).reshape(P, -1)
    for name in ("cmp_pos_k", "cmp_pos_v"):
        laid[name] = np.asarray(inputs[name])[0].T
    for name in _INS:
        give(f"in_{name}_dram", laid[name])
    half = DH // 2
    give("inv_freq_dram", np.power(np.float32(10000.0), -np.arange(half, dtype=np.float32) / half).astype(np.float32))
    norms = [(inputs[f"ln_{k}_g"][i], inputs[f"ln_{k}_b"][i]) for i in range(DEPTH) for k in ("mix", "ffn")]
    give("ln_by_feature_dram", np.stack([np.stack([np.asarray(v).reshape(KT, P).T for v in n], 1) for n in norms], 1))
    give("end_positions_dram", np.tile(np.asarray(inputs["positions"])[0, CMPB - 1::STRIDE], NG).reshape(NCG, 1))
    args.append(nc.dram_tensor("out_dram", (1, SEQ, D), F32, kind="ExternalOutput").ap())
    trunk(nc, *args, stop=STOP)
    r = run(nc, [arrays], core_ids=[0])
    return r.results[0]["out_dram"]
```
